# Optimizing a Trainium2 kernel written in Bass

```python
import math
import jax, jax.numpy as jnp
from jax import lax
import numpy as np

D_MODEL = 1024
BATCH = 1
SEQ = 256
DEPTH = 2

MIX_WIDTH = D_MODEL
ATTN_HEADS = 8
HEAD_DIM = 64
ATTN_WIDTH = ATTN_HEADS * HEAD_DIM
DILATED_PATTERNS = ((128, 1), (512, 4), (2048, 16))
QUERY_BLOCK = 128
ROPE_THETA = 500000.0
ROPE_DIM = HEAD_DIM // 4
POOL_WINDOWS = (2, 4, 8, 16)
POOL_GROUPS = len(POOL_WINDOWS)
POOL_WIDTH = MIX_WIDTH - ATTN_WIDTH
POOL_GROUP_DIM = POOL_WIDTH // POOL_GROUPS
AB_IN_WIDTH = 3 * ATTN_WIDTH + POOL_WIDTH
SGU_CHUNK = 128
SGU_GROUPS = 8
SGU_WIDTH = MIX_WIDTH
SGU_GROUP_DIM = SGU_WIDTH // SGU_GROUPS
PEER_HEADS = 8
PEER_N_KEYS = 128
PEER_EXPERTS = PEER_N_KEYS * PEER_N_KEYS
PEER_TOPK = 16
PEER_QUERY_DIM = 256
PEER_HALF_DIM = PEER_QUERY_DIM // 2
PEER_TOKEN_BLOCK = 512
N_EVEN = (DEPTH + 1) // 2
N_ODD = DEPTH // 2
RMS_EPS = 1e-6
NEG_INF = -1e30

kernel_name = "hybrid_dilated_pool_sgu_peer_encoder"

def rms_norm(x, g):
    x32 = x.astype(jnp.float32)
    y = x32 * lax.rsqrt(jnp.mean(x32 * x32, axis=-1, keepdims=True) + RMS_EPS)
    return (y * g.astype(jnp.float32)).astype(x.dtype)

def partial_rotary(t):
    S = t.shape[1]
    half = ROPE_DIM // 2
    pos = jnp.arange(S, dtype=jnp.float32)
    inv_freq = ROPE_THETA ** (-jnp.arange(0, ROPE_DIM, 2, dtype=jnp.float32) / ROPE_DIM)
    ang = pos[:, None] * inv_freq[None, :]
    cos = jnp.cos(ang)[None, :, None, :]
    sin = jnp.sin(ang)[None, :, None, :]
    tr = t[..., :ROPE_DIM].astype(jnp.float32)
    t1, t2 = tr[..., :half], tr[..., half:]
    rot = jnp.concatenate([t1 * cos - t2 * sin, t2 * cos + t1 * sin], axis=-1)
    return jnp.concatenate([rot.astype(t.dtype), t[..., ROPE_DIM:]], axis=-1)

def banded_attention(q, k, v, half):
    N, L, H, dh = q.shape
    bq = math.gcd(L, QUERY_BLOCK)
    nb = L // bq
    kw = bq + 2 * half
    pad = ((0, 0), (half, half), (0, 0), (0, 0))
    kp = jnp.pad(k, pad)
    vp = jnp.pad(v, pad)
    kidx = (jnp.arange(nb) * bq)[:, None] + jnp.arange(kw)[None, :]
    kb = kp[:, kidx]
    vb = vp[:, kidx]
    qb = q.reshape(N, nb, bq, H, dh)
    s = jnp.einsum('nbqhd,nbkhd->nbhqk', qb, kb).astype(jnp.float32) * (dh ** -0.5)
    rel = jnp.arange(kw)[None, :] - half - jnp.arange(bq)[:, None]
    kpos = kidx - half
    valid = (jnp.abs(rel) <= half)[None] & ((kpos >= 0) & (kpos < L))[:, None, :]
    s = jnp.where(valid[None, :, None], s, NEG_INF)
    lse = jax.nn.logsumexp(s, axis=-1)
    p = jnp.exp(s - lse[..., None])
    o = jnp.einsum('nbhqk,nbkhd->nbqhd', p, vb.astype(jnp.float32))
    return o.reshape(N, L, H, dh), lse.transpose(0, 1, 3, 2).reshape(N, L, H)

def dilated_attention(q, k, v):
    B, S, H, dh = q.shape
    outs, lses = [], []
    for window, dil in DILATED_PATTERNS:
        half = window // (2 * dil)
        L = S // dil

        def strided(t):
            return t.reshape(B, L, dil, H, dh).transpose(0, 2, 1, 3, 4).reshape(B * dil, L, H, dh)

        o, lse = banded_attention(strided(q), strided(k), strided(v), half)
        outs.append(o.reshape(B, dil, L, H, dh).transpose(0, 2, 1, 3, 4).reshape(B, S, H, dh))
        lses.append(lse.reshape(B, dil, L, H).transpose(0, 2, 1, 3).reshape(B, S, H))
    w = jax.nn.softmax(jnp.stack(lses, axis=-1), axis=-1)
    out = jnp.einsum('bshdp,bshp->bshd', jnp.stack(outs, axis=-1), w)
    return out.reshape(B, S, H * dh).astype(q.dtype)

def multiscale_pool(u, w, scale):
    B, S, _ = u.shape
    ug = u.astype(jnp.float32).reshape(B, S, POOL_GROUPS, POOL_GROUP_DIM)
    c = jnp.pad(jnp.cumsum(ug, axis=1), ((0, 0), (1, 0), (0, 0), (0, 0)))
    pos = jnp.arange(S)
    pooled = []
    for g, win in enumerate(POOL_WINDOWS):
        lo = jnp.clip(pos - win // 2, 0, S)
        hi = jnp.clip(pos + win - win // 2, 0, S)
        cnt = (hi - lo).astype(jnp.float32)
        pooled.append((c[:, hi, g] - c[:, lo, g]) / cnt[None, :, None])
    pooled = jnp.stack(pooled, axis=2)
    mixed = jnp.einsum('bsgc,gcd->bsgd', pooled - ug, w.astype(jnp.float32))
    return (mixed.reshape(B, S, POOL_WIDTH) * scale.astype(jnp.float32)).astype(u.dtype)

def spatial_gating_mlp(h, w_in, norm_g, w_s, b_s, w_out):
    B, S, _ = h.shape
    z = jax.nn.gelu(h @ w_in)
    u, v = z[..., :SGU_WIDTH], z[..., SGU_WIDTH:]
    v = rms_norm(v, norm_g)
    nc = S // SGU_CHUNK
    vc = v.reshape(B, nc, SGU_CHUNK, SGU_GROUPS, SGU_GROUP_DIM)
    mixed = jnp.einsum('gpq,bnqgc->bnpgc', w_s, vc) + b_s.T[None, None, :, :, None]
    gated = u * mixed.reshape(B, S, SGU_WIDTH)
    return gated @ w_out

def peer(h, w_q, sub_keys, w_down, w_up):
    B, S, D = h.shape
    T = B * S
    ht = h.reshape(T, D)
    q = (ht @ w_q).reshape(T, PEER_HEADS, 2, PEER_HALF_DIM)
    scores = jnp.einsum('thic,hikc->thik', q, sub_keys).astype(jnp.float32)
    sv, si = lax.top_k(scores, PEER_TOPK)
    cand = sv[:, :, 0, :, None] + sv[:, :, 1, None, :]
    best, ci = lax.top_k(cand.reshape(T, PEER_HEADS, PEER_TOPK * PEER_TOPK), PEER_TOPK)
    i1 = jnp.take_along_axis(si[:, :, 0], ci // PEER_TOPK, axis=-1)
    i2 = jnp.take_along_axis(si[:, :, 1], ci % PEER_TOPK, axis=-1)
    expert = (i1 * PEER_N_KEYS + i2).reshape(T, PEER_HEADS * PEER_TOPK)
    gate = jax.nn.softmax(best, axis=-1).reshape(T, PEER_HEADS * PEER_TOPK)
    blk = math.gcd(T, PEER_TOKEN_BLOCK)
    nblk = T // blk

    def expert_block(args):
        xb, eb, gb = args
        hid = jax.nn.gelu(jnp.einsum('cd,ckd->ck', xb, w_down[eb]).astype(jnp.float32))
        return jnp.einsum('ck,ckd->cd', (gb * hid).astype(xb.dtype), w_up[eb])

    out = lax.map(expert_block, (ht.reshape(nblk, blk, D),
                                 expert.reshape(nblk, blk, PEER_HEADS * PEER_TOPK),
                                 gate.reshape(nblk, blk, PEER_HEADS * PEER_TOPK)))
    return out.reshape(B, S, D)

def setup_inputs(seed: int = 0) -> dict:
    key = jax.random.key(seed)
    ks = jax.random.split(key, 20)
    f32 = jnp.float32

    def nrm(k, shape, scale):
        return jax.random.normal(k, shape, f32) * scale

    return {
        "x": nrm(ks[0], (BATCH, SEQ, D_MODEL), 1.0),
        "norm_mix": 1.0 + nrm(ks[1], (DEPTH, D_MODEL), 0.02),
        "norm_ffn": 1.0 + nrm(ks[2], (DEPTH, D_MODEL), 0.02),
        "norm_final": 1.0 + nrm(ks[3], (D_MODEL,), 0.02),
        "ab_w_in": nrm(ks[4], (N_EVEN, D_MODEL, AB_IN_WIDTH), D_MODEL ** -0.5),
        "ab_w_out": nrm(ks[5], (N_EVEN, MIX_WIDTH, D_MODEL), MIX_WIDTH ** -0.5),
        "pool_w": nrm(ks[6], (N_EVEN, POOL_GROUPS, POOL_GROUP_DIM, POOL_GROUP_DIM), POOL_GROUP_DIM ** -0.5),
        "pool_scale": 1.0 + nrm(ks[7], (N_EVEN, POOL_WIDTH), 0.02),
        "c_w_in": nrm(ks[8], (N_ODD, D_MODEL, 2 * SGU_WIDTH), D_MODEL ** -0.5),
        "c_norm": 1.0 + nrm(ks[9], (N_ODD, SGU_WIDTH), 0.02),
        "c_w_s": nrm(ks[10], (N_ODD, SGU_GROUPS, SGU_CHUNK, SGU_CHUNK), SGU_CHUNK ** -0.5),
        "c_b_s": 1.0 + nrm(ks[11], (N_ODD, SGU_GROUPS, SGU_CHUNK), 0.02),
        "c_w_out": nrm(ks[12], (N_ODD, SGU_WIDTH, D_MODEL), SGU_WIDTH ** -0.5),
        "peer_w_q": nrm(ks[13], (DEPTH, D_MODEL, PEER_HEADS * PEER_QUERY_DIM), D_MODEL ** -0.5),
        "peer_sub_keys": nrm(ks[14], (DEPTH, PEER_HEADS, 2, PEER_N_KEYS, PEER_HALF_DIM), PEER_HALF_DIM ** -0.5),
        "peer_w_down": nrm(ks[15], (DEPTH, PEER_EXPERTS, D_MODEL), D_MODEL ** -0.5),
        "peer_w_up": nrm(ks[16], (DEPTH, PEER_EXPERTS, D_MODEL), PEER_HEADS ** -0.5),
    }

def reference(x, norm_mix, norm_ffn, norm_final, ab_w_in, ab_w_out, pool_w, pool_scale,
              c_w_in, c_norm, c_w_s, c_b_s, c_w_out,
              peer_w_q, peer_sub_keys, peer_w_down, peer_w_up):
    B, S, _ = x.shape
    for layer in range(DEPTH):
        j = layer // 2
        h = rms_norm(x, norm_mix[layer])
        if layer % 2 == 0:
            proj = h @ ab_w_in[j]
            q = proj[..., :ATTN_WIDTH].reshape(B, S, ATTN_HEADS, HEAD_DIM)
            k = proj[..., ATTN_WIDTH:2 * ATTN_WIDTH].reshape(B, S, ATTN_HEADS, HEAD_DIM)
            v = proj[..., 2 * ATTN_WIDTH:3 * ATTN_WIDTH].reshape(B, S, ATTN_HEADS, HEAD_DIM)
            p_in = proj[..., 3 * ATTN_WIDTH:]
            a_out = dilated_attention(partial_rotary(q), partial_rotary(k), v)
            b_out = multiscale_pool(p_in, pool_w[j], pool_scale[j])
            mix = jnp.concatenate([a_out, b_out], axis=-1) @ ab_w_out[j]
        else:
            mix = spatial_gating_mlp(h, c_w_in[j], c_norm[j], c_w_s[j], c_b_s[j], c_w_out[j])
        x = x + mix
        x = x + peer(rms_norm(x, norm_ffn[layer]), peer_w_q[layer], peer_sub_keys[layer],
                     peer_w_down[layer], peer_w_up[layer])
    return rms_norm(x, norm_final)


_drawn_inputs = setup_inputs


def setup_inputs(seed=0):
    import zlib

    import numpy as np

    out = dict(_drawn_inputs(seed))
    spreads = {}
    factors = {}
    for name, (base, spread) in spreads.items():
        noise = np.random.default_rng([zlib.crc32(name.encode()), seed]).standard_normal(out[name].shape)
        drawn = base * np.exp(spread * noise) if base else spread * noise
        out[name] = __import__('jax').numpy.asarray(drawn.astype(out[name].dtype))
    for name, factor in factors.items():
        out[name] = (out[name] * factor).astype(out[name].dtype)
    return out
```

```python
from contextlib import ExitStack

import numpy as np

import concourse.bass as bass
from concourse import mybir

F32 = mybir.dt.float32
F32R = mybir.dt.float32r
I32 = mybir.dt.int32
U32 = mybir.dt.uint32
ALU = mybir.AluOpType
ACT = mybir.ActivationFunctionType
AX = mybir.AxisListType

P = 128
LAYERS = 2
SEQ = 256
TILES = SEQ // P
DM = 1024
DC = DM // P
PROJ = 2048
NB = PROJ // 512
EPS = 1e-6

HEADS = 8
HD = 64
ROT = HD // 8
WINDOWS = (2, 4, 8, 16)
PATTERNS = ((128, 1), (512, 4), (2048, 16))
GROUPS = 8

RH = 8
HALVES = 2 * RH
KEYS = 128
TOPK = 16
SEGS = ((0, 1, 16), (1, 2, 8), (2, 4, 5), (4, 8, 3), (8, 16, 1))
CAND = sum((a1 - a0) * nb for a0, a1, nb in SEGS)
LOWEST = -3.0e38

BLOCKS = KEYS
RAW = 4
WHI = 4
WLO = 2
GHS = 4
TOK = 4
TGROUPS = SEQ // TOK
EXP_AT = 72
IDS_AT = 84

W_IN = 0
W_OUT = 0
W_Q = 8192
PROJ_AT = 16384
QKT_AT = 20480
VN_AT = 20480
PR_AT = 22528
WS_AT = 22528
CN_AT = 23552
BS_AT = 24576
PT_AT = 26624
SUBK_AT = 26624
POOLED_AT = 28672
SC_AT = 28672
MIXT_AT = 30720
QT_AT = 0
EQ_AT = 21824
SV_AT = 23552
SI_AT = 24064
SIF_AT = 24576
CD_AT = 25088
PAY_AT = 25520
assert EQ_AT + 32 * CAND <= SV_AT and PAY_AT + RH * CAND <= SUBK_AT and IDS_AT * SEQ <= EQ_AT
BEST_AT, CIF_AT, IDF_AT, CI_AT = 1024, 1280, 1536, 1792


def build_trunk(nc, x_d, gam_d, gfin_d, tab_d, ident_d, iota_d, iotac_d, lncount_d, poolm_d, poolw_d,
                pscale_d, w_in_d, w_out_d, ws_d, bs_d, cnorm_d, wq_d, subk_d, wd_d, wu_d, out_d):
    ctx = ExitStack()
    with ctx:
        def sb(name, shape, dt):
            return ctx.enter_context(nc.sbuf_tensor(name, shape, dt))

        def sem(name):
            return ctx.enter_context(nc.semaphore(name))

        arena = sb("arena", [P, BLOCKS * SEQ], F32)
        xs = sb("xs", [P, TILES, DM], F32)
        hT = sb("hT", [P, DC * SEQ], F32)
        hT_hi = sb("hT_hi", [P, DC * SEQ], F32R)
        hT_lo = sb("hT_lo", [P, DC * SEQ], F32R)
        raw = sb("raw", [P, RAW, DM], F32)
        w_hi = sb("w_hi", [P, WHI * DM], F32R)
        w_lo = sb("w_lo", [P, WLO, DM], F32R)
        ident = sb("ident", [P, P], F32)
        iota = sb("iota", [P, P], F32)
        iotac = sb("iotac", [P, CAND], F32)
        gam = sb("gam", [P, 2 * LAYERS, DC], F32)
        tab = sb("tab", [P, 2, TILES, ROT], F32)
        pscale = sb("pscale", [P, len(WINDOWS)], F32)
        sumsq = sb("sumsq", [P, TILES], F32)
        meansq = sb("meansq", [P, TILES], F32)
        std = sb("std", [P, TILES], F32)
        rinv = sb("rinv", [P, TILES], F32)
        rtmp = sb("rtmp", [P, TILES], F32)
        rot = sb("rot", [P, 4, 2 * HEADS, ROT], F32)
        rowmax = sb("rowmax", [P, HEADS, TILES], F32)
        rowsum = sb("rowsum", [P, HEADS, TILES], F32)
        rowinv = sb("rowinv", [P, HEADS, TILES], F32)
        gsum = sb("gsum", [P, 2 * TILES, RH], F32)
        g_hi = sb("g_hi", [P, SEQ], F32R)
        ps = ctx.enter_context(nc.psum_tensor("ps", [P, 8, 512], F32))

        def at(start, *dims):
            size = int(np.prod(dims))
            v = arena[:, start:start + size]
            if len(dims) == 1:
                return v
            names = "abcd"[:len(dims)]
            return v.rearrange(f"p ({' '.join(names)}) -> p {' '.join(names)}",
                               **{k: d for k, d in zip(names, dims)})

        H = arena[:, :].rearrange("p (i t) -> p i t", t=SEQ)
        w_in = at(W_IN, DC, PROJ)
        w_out = at(W_OUT, DC, DM)
        w_q = at(W_Q, DC, PROJ)
        proj = at(PROJ_AT, TILES, PROJ)
        u_sb = at(PROJ_AT, TILES, DM)
        v_sb = at(PROJ_AT + TILES * DM, TILES, DM)
        vn = at(VN_AT, TILES, DM)
        qkT = at(QKT_AT, DC, SEQ)
        probs = at(PR_AT, HEADS, TILES * SEQ)
        probsT = at(PT_AT, HEADS, TILES * SEQ)
        poolm = at(PT_AT, TILES, len(WINDOWS), SEQ)
        pooledT = at(POOLED_AT, len(WINDOWS), SEQ)
        ws = at(WS_AT, GROUPS, P)
        cnorm = at(CN_AT, DM)
        bs = at(BS_AT, GROUPS)
        mixT = at(MIXT_AT, DC, SEQ)
        hn = at(MIXT_AT, TILES, DM)
        qT = at(QT_AT, HALVES, SEQ)
        subk = at(SUBK_AT, HALVES, KEYS)
        scores = at(SC_AT, TILES, HALVES * KEYS)
        sv = at(SV_AT, TILES, HALVES, TOPK)
        si = arena[:, SI_AT:SI_AT + TILES * HALVES * TOPK].bitcast(U32).rearrange(
            "p (a b c) -> p a b c", a=TILES, b=HALVES)
        sif = at(SIF_AT, TILES, RH, 2, TOPK)
        cand = at(CD_AT, RH, CAND)
        pay = at(PAY_AT, RH, CAND)
        eq = at(EQ_AT, 2 * TOPK, CAND)
        lncount = raw[:, RAW - 1, 0:TILES * SEQ]
        poolw = raw[:, RAW - 1, 512:1024].rearrange("p (g c) -> p g c", c=P)

        hTc = hT[:, :].rearrange("p (c t) -> p c t", t=SEQ)
        i1T, i2T = hT[:, 0:SEQ], hT[:, SEQ:2 * SEQ]
        gT, g_lo = hT[:, 2 * SEQ:3 * SEQ], hT[:, 3 * SEQ:4 * SEQ]
        best = hT[:, BEST_AT:BEST_AT + TILES * P].rearrange("p (t h k) -> p t h k", t=TILES, h=RH)
        cif = hT[:, CIF_AT:CIF_AT + TILES * P].rearrange("p (t n) -> p t n", t=TILES)
        idf = hT[:, IDF_AT:IDF_AT + TILES * P].rearrange("p (t n) -> p t n", t=TILES)
        ci = hT[:, CI_AT:CI_AT + TILES * P].bitcast(U32).rearrange("p (t h k) -> p t h k", t=TILES, h=RH)
        idi = hT[:, CIF_AT:CIF_AT + SEQ].bitcast(I32)
        idk = hT[:, CI_AT:CI_AT + SEQ].bitcast(I32)

        hh = hT_hi[:, :].rearrange("p (c t) -> p c t", t=SEQ)
        hl = hT_lo[:, :].rearrange("p (c t) -> p c t", t=SEQ)
        whs = w_hi[:, :].rearrange("p (s n) -> p s n", s=WHI)
        oh = w_hi[:, 0:3 * 2 * TOK * P].rearrange("p (k s t i) -> p k s t i", k=3, s=2, t=TOK)
        oh2, oh1h, oh1l = oh[:, 0], oh[:, 1], oh[:, 2]

        x_loaded, consts_loaded, tabs_loaded = sem("x_loaded"), sem("consts_loaded"), sem("tabs_loaded")
        wbig_loaded = [sem(f"wbig_loaded{q}") for q in range(4)]
        win1_loaded = [sem(f"win1_loaded{q}") for q in range(4)]
        wout_loaded, subk_loaded = sem("wout_loaded"), sem("subk_loaded")
        sgu_loaded, gfin_loaded = sem("sgu_loaded"), sem("gfin_loaded")
        raw_full = [sem(f"raw_full{s}") for s in range(RAW)]
        out_stored = sem("out_stored")
        sumsq_done, ms_done, std_done = sem("sumsq_done"), sem("ms_done"), sem("std_done")
        hn_done, hT_psum, hT_act, hT_dve = sem("hn_done"), sem("hT_psum"), sem("hT_act"), sem("hT_dve")
        hi_done, lo_done = sem("hT_hi_done"), sem("hT_lo_done")
        x_ready = sem("x_ready")
        proj_psum, proj_sb = sem("proj_psum"), sem("proj_sb")
        pool_psum, pooled_sb, poolmix_psum, mixT_pool = (
            sem("pool_psum"), sem("pooled_sb"), sem("poolmix_psum"), sem("mixT_pool"))
        rot_done, qkT_psum, qkT_sb = sem("rot_done"), sem("qkT_psum"), sem("qkT_sb")
        s_psum, nmax_done, exp_done, p_done = sem("s_psum"), sem("nmax_done"), sem("exp_done"), sem("p_done")
        pT_psum, pT_sb, pv_psum, mixT_attn = sem("pT_psum"), sem("pT_sb"), sem("pv_psum"), sem("mixT_attn")
        vn_done, sgu_psum, gated_done = sem("vn_done"), sem("sgu_psum"), sem("gated_done")
        gT_psum, gT_sb = sem("gT_psum"), sem("gT_sb")
        mix_psum = sem("mix_psum")
        q_psum, qT_sb, sc_psum, sc_sb = sem("q_psum"), sem("qT_sb"), sem("sc_psum"), sem("sc_sb")
        best_done, gexp_done, idg_done, idg_psum = (
            sem("best_done"), sem("gexp_done"), sem("idg_done"), sem("idg_psum"))
        whi_done, wlo_pool, wlo_dve, w_used = sem("whi_done"), sem("wlo_pool"), sem("wlo_dve"), sem("w_used")
        h_done, ghhi_done, ghlo_done = sem("h_done"), sem("ghhi_done"), sem("ghlo_done")
        oh_built, g_mm, gmul_done = sem("oh_built"), sem("g_mm"), sem("gmul_done")
        dve_step, act_step = sem("dve_step"), sem("act_step")

        def blocks(eng, body, first, last):
            with eng.Fori(first // RAW, last // RAW) as i:
                for j in range(RAW):
                    body(i * RAW + j, j)

        block = ctx.enter_context(nc.Block())

        @block.sync
        def _(sp):
            sp.dma_start(xs[:, :, :], x_d).then_inc(x_loaded, 16)
            sp.dma_start(ident[:, :], ident_d).then_inc(consts_loaded, 16)
            sp.dma_start(gam[:, :, :], gam_d).then_inc(consts_loaded, 16)

            def quarter(dst, src, q):
                c = slice(q * DC // 4, (q + 1) * DC // 4)
                sp.dma_start(dst[:, c, :], src[:, c, :]).then_inc(wbig_loaded[q], 16)

            for q in range(4):
                quarter(w_in, w_in_d[0], q)
            sp.dma_start(tab[:, :, :, :], tab_d).then_inc(tabs_loaded, 16)
            sp.dma_start(pscale[:, :], pscale_d).then_inc(tabs_loaded, 16)
            sp.dma_start(iota[:, :], iota_d).then_inc(tabs_loaded, 16)
            sp.dma_start(iotac[:, :], iotac_d).then_inc(tabs_loaded, 16)
            sp.dma_start(poolm, poolm_d).then_inc(tabs_loaded, 16)
            sp.dma_start(poolw, poolw_d).then_inc(tabs_loaded, 16)
            sp.dma_start(lncount, lncount_d).then_inc(tabs_loaded, 16)
            for l in range(LAYERS):
                if l == 1:
                    sp.wait_ge(ghlo_done, BLOCKS)
                    sp.dma_start(ws, ws_d).then_inc(sgu_loaded, 16)
                    sp.dma_start(bs, bs_d).then_inc(sgu_loaded, 16)
                    sp.dma_start(cnorm, cnorm_d).then_inc(sgu_loaded, 16)
                sp.wait_ge(proj_psum, 2 * NB * (l + 1))
                sp.dma_start(w_out, w_out_d[l]).then_inc(wout_loaded, 16)
                if l == 0:
                    sp.wait_ge(mixT_attn, HEADS // 2)
                    sp.wait_ge(mixT_pool, len(WINDOWS))
                else:
                    sp.wait_ge(gT_sb, DC // 2)
                for q in range(4):
                    quarter(w_q, wq_d[l], q)
                sp.dma_start(subk, subk_d[l]).then_inc(subk_loaded, 16)

                def load(src, used, base, b, s):
                    sp.wait_ge(used, base + b - RAW + 1)
                    sp.dma_start(raw[:, s, :], src[l, bass.ds(b, 1)].rearrange("b p n -> p (b n)")
                                 ).then_inc(raw_full[s], 16)

                for phase, (src, used, before) in enumerate(((wd_d, wlo_pool, wlo_dve),
                                                             (wu_d, wlo_dve, wlo_pool))):
                    for s in range(RAW):
                        if phase or l:
                            sp.wait_ge(before, (l + phase) * BLOCKS - RAW + 1 + s)
                        sp.dma_start(raw[:, s, :], src[l, s]).then_inc(raw_full[s], 16)
                    blocks(sp, lambda b, s: load(src, used, l * BLOCKS, b, s), RAW, BLOCKS)
            sp.wait_ge(ghlo_done, LAYERS * BLOCKS)
            sp.dma_start(cnorm, gfin_d).then_inc(gfin_loaded, 16)
            sp.wait_ge(hn_done, 2 * (2 * LAYERS + 1))
            sp.dma_start(out_d, hn).then_inc(out_stored, 16)
            sp.wait_ge(out_stored, 16)

        @block.gpsimd
        def _(pool):
            for l in range(LAYERS):
                def low_part(b, s):
                    n = b + l * 2 * BLOCKS
                    pool.wait_ge(whi_done, n + 1)
                    pool.wait_ge(w_used, n - WLO + 1)
                    nc.gpsimd.tensor_tensor(w_lo[:, s % WLO, :], raw[:, s, :],
                                            whs[:, s].bitcast(F32), ALU.subtract).then_inc(wlo_pool, 1)

                for b in range(RAW):
                    if l == 0 and b < WLO:
                        pool.wait_ge(whi_done, b + 1)
                        nc.gpsimd.tensor_tensor(w_lo[:, b, :], raw[:, b, :], whs[:, b].bitcast(F32),
                                                ALU.subtract).then_inc(wlo_pool, 1)
                    else:
                        low_part(b, b)
                blocks(pool, low_part, RAW, BLOCKS)
                if l == 0:
                    pool.wait_ge(ghlo_done, BLOCKS // 2)
                    for q in range(4):
                        c = slice(q * DC // 4, (q + 1) * DC // 4)
                        pool.dma_start(w_in[:, c, :], w_in_d[1][:, c, :]).then_inc(win1_loaded[q], 16)

        @block.scalar
        def _(act):
            steps = [0]
            norms = [0]

            def link(ins):
                steps[0] += 1
                ins.then_inc(act_step, 1)
                act.wait_ge(act_step, steps[0])

            def norm_stats(src, junk):
                norms[0] += 1
                for t in range(TILES):
                    nc.scalar.activation(junk[:, t, :], src[:, t, :], ACT.Square,
                                         accum_out=sumsq[:, t:t + 1]).then_inc(sumsq_done, 1)
                act.wait_ge(ms_done, norms[0])
                nc.scalar.activation(std[:, :], meansq[:, :], ACT.Sqrt).then_inc(std_done, 1)

            def evacuate_hT(k, bank):
                for c in range(DC // 2):
                    act.wait_ge(hT_psum, k * DC // 2 + c // 2 + 1)
                    nc.scalar.activation(hTc[:, c, :], ps[:, bank + c // 2, c % 2 * SEQ:(c % 2 + 1) * SEQ],
                                         ACT.Copy, scale=gam[:, k, c:c + 1]).then_inc(hT_act, 1)

            act.wait_ge(x_loaded, 16)
            for l in range(LAYERS):
                if l:
                    act.wait_ge(x_ready, 8 * l)
                norm_stats(xs, hn)
                if l == 0:
                    act.wait_ge(consts_loaded, 32)
                evacuate_hT(2 * l, 0)
                if l == 0:
                    for i in range(2 * NB):
                        t, nb = divmod(i, NB)
                        act.wait_ge(proj_psum, i + 1)
                        nc.scalar.activation(proj[:, t, nb * 512:(nb + 1) * 512],
                                             ps[:, nb if t else NB + nb, :], ACT.Copy).then_inc(proj_sb, 1)
                    for g in range(len(WINDOWS)):
                        act.wait_ge(pool_psum, g + 1)
                        nc.scalar.activation(pooledT[:, g, :], ps[:, 4 + g, 0:SEQ],
                                             ACT.Copy).then_inc(pooled_sb, 1)
                    act.wait_ge(tabs_loaded, 112)
                    for g in range(len(WINDOWS)):
                        act.wait_ge(poolmix_psum, g + 1)
                        nc.scalar.activation(mixT[:, 4 + g, :], ps[:, 4 + g, SEQ:2 * SEQ], ACT.Copy,
                                             scale=pscale[:, g:g + 1]).then_inc(mixT_pool, 1)

                    def take_probsT(h):
                        act.wait_ge(pT_psum, h + 1)
                        nc.scalar.activation(probsT[:, h, :], ps[:, h, :], ACT.Copy).then_inc(pT_sb, 1)

                    for h in range(HEADS):
                        act.wait_ge(nmax_done, h + 1)
                        for t in range(TILES):
                            p = probs[:, h, t * SEQ:(t + 1) * SEQ]
                            nc.scalar.activation(p, p, ACT.Exp, bias=rowmax[:, h, t:t + 1],
                                                 accum_out=rowsum[:, h, t:t + 1]).then_inc(exp_done, 1)
                        if h >= 2:
                            take_probsT(h - 2)
                    take_probsT(HEADS - 2)
                    take_probsT(HEADS - 1)
                    for j in range(HEADS // 2):
                        act.wait_ge(pv_psum, j + 1)
                        nc.scalar.activation(mixT[:, j, :], ps[:, j, 0:SEQ], ACT.Copy).then_inc(mixT_attn, 1)
                else:
                    for i in range(2 * NB):
                        t, nb = divmod(i, NB)
                        act.wait_ge(proj_psum, 2 * NB + i + 1)
                        dst = (u_sb if nb < 2 else v_sb)[:, t, nb % 2 * 512:(nb % 2 + 1) * 512]
                        ins = nc.scalar.activation(dst, ps[:, nb if t else NB + nb, :], ACT.Gelu_apprx_tanh)
                        ins.then_inc(proj_sb, 1)
                    act.wait_ge(proj_sb, 4 * NB)
                    norm_stats(v_sb, vn)
                    for i in range(DC // 2):
                        act.wait_ge(gT_psum, i + 1)
                        nc.scalar.activation(mixT[:, 2 * i:2 * i + 2, :],
                                             ps[:, i, :].rearrange("p (c t) -> p c t", t=SEQ),
                                             ACT.Copy).then_inc(gT_sb, 1)

                act.wait_ge(x_ready, 8 * l + 4)
                norm_stats(xs, hn)
                evacuate_hT(2 * l + 1, 4)
                act.wait_ge(hT_act, (2 * l + 2) * DC // 2)
                act.wait_ge(hT_dve, (2 * l + 2) * DC // 2)
                nc.scalar.activation(hT_hi[:, :], hT[:, :], ACT.Copy).then_inc(hi_done, 1)
                for i in range(HALVES // 2):
                    act.wait_ge(q_psum, l * HALVES // 2 + i + 1)
                    nc.scalar.activation(qT[:, 2 * i:2 * i + 2, :],
                                         ps[:, i, :].rearrange("p (c t) -> p c t", t=SEQ),
                                         ACT.Copy).then_inc(qT_sb, 1)
                for i in range(8):
                    act.wait_ge(sc_psum, 8 * l + i + 1)
                    nc.scalar.activation(scores[:, i // 4, i % 4 * 512:(i % 4 + 1) * 512],
                                         ps[:, i, :], ACT.Copy).then_inc(sc_sb, 1)

                def high_part(n, s, first=False):
                    act.wait_ge(raw_full[s], (n - s) * (16 // RAW) + 16)
                    if not first:
                        act.wait_ge(w_used, n - WHI + 1)
                    nc.scalar.activation(whs[:, s], raw[:, s, :], ACT.Copy).then_inc(whi_done, 1)

                def take_hidden(b, s):
                    act.wait_ge(w_used, b + 1 + 2 * l * BLOCKS)
                    nc.scalar.activation(arena[:, bass.ds(b * SEQ, SEQ)], ps[:, s, 0:SEQ],
                                         ACT.Gelu_apprx_tanh).then_inc(h_done, 1)

                def down(b, s):
                    high_part(b + 2 * l * BLOCKS, s)
                    take_hidden(b - 2, (s - 2) % RAW)

                for b in range(RAW):
                    high_part(b + 2 * l * BLOCKS, b, first=l == 0)
                    if b >= 2:
                        take_hidden(b - 2, b - 2)
                blocks(act, down, RAW, EXP_AT)
                act.wait_ge(best_done, l + 1)
                bb = hT[:, BEST_AT:BEST_AT + TILES * P]
                nc.scalar.activation(bb, bb, ACT.Exp).then_inc(gexp_done, 1)
                blocks(act, down, EXP_AT, IDS_AT)
                act.wait_ge(idg_done, l + 1)
                blocks(act, down, IDS_AT, BLOCKS)
                take_hidden(BLOCKS - 2, RAW - 2)
                take_hidden(BLOCKS - 1, RAW - 1)

                def up(b, s):
                    n = b + (2 * l + 1) * BLOCKS
                    high_part(n, s)
                    nc.scalar.activation(hh[:, s, :], arena[:, bass.ds(b * SEQ, SEQ)],
                                         ACT.Copy).then_inc(ghhi_done, 1)

                act.wait_ge(gmul_done, (l + 1) * TGROUPS)
                act.wait_ge(g_mm, (l + 1) * TGROUPS)
                blocks(act, up, 0, BLOCKS)
            act.wait_ge(x_ready, 8 * LAYERS)
            norm_stats(xs, hn)

        @block.tensor
        def _(pe):
            def mm(out, lhsT, rhs, start=True, stop=True, shared=False):
                return nc.tensor.matmul(out, lhsT, rhs, start=start, stop=stop, skip_group_check=shared)

            def transpose_tokens(src, bank, done):
                for i in range(DC // 2):
                    for c in (2 * i, 2 * i + 1):
                        for t in range(TILES):
                            o = (c % 2) * SEQ + t * P
                            last = nc.tensor.transpose(ps[:, bank + i, o:o + P],
                                                       src[:, t, c * P:(c + 1) * P], ident[:, :])
                    last.then_inc(done, 1)

            pe.wait_ge(consts_loaded, 32)
            for l in range(LAYERS):
                pe.wait_ge(hn_done, 4 * l + 2)
                transpose_tokens(hn, 0, hT_psum)
                pe.wait_ge(hT_act, (2 * l + 1) * DC // 2)
                pe.wait_ge(hT_dve, (2 * l + 1) * DC // 2)
                for t in range(TILES):
                    for c in range(DC):
                        if t == 0 and c % 2 == 0:
                            pe.wait_ge((win1_loaded if l else wbig_loaded)[c // 2], 16)
                        for nb in range(NB):
                            last = mm(ps[:, nb if t else NB + nb, :], hTc[:, c, t * P:(t + 1) * P],
                                      w_in[:, c, nb * 512:(nb + 1) * 512], c == 0, c == DC - 1)
                            if c == DC - 1:
                                last.then_inc(proj_psum, 1)
                if l == 0:
                    pe.wait_ge(tabs_loaded, 112)
                    pe.wait_ge(proj_sb, 2 * NB)
                    for g in range(len(WINDOWS)):
                        o = 3 * 512 + g * P
                        for t in range(TILES):
                            last = mm(ps[:, 4 + g, 0:SEQ], proj[:, t, o:o + P], poolm[:, t, g, :],
                                      t == 0, t == TILES - 1)
                        last.then_inc(pool_psum, 1)
                    pe.wait_ge(rot_done, TILES)
                    transpose_tokens(proj, 0, qkT_psum)
                    for g in range(len(WINDOWS)):
                        pe.wait_ge(pooled_sb, g + 1)
                        mm(ps[:, 4 + g, SEQ:2 * SEQ], poolw[:, g, :], pooledT[:, g, :]
                           ).then_inc(poolmix_psum, 1)
                    pe.wait_ge(qkT_sb, DC // 2)
                    for h in range(HEADS):
                        if h == 4:
                            pe.wait_ge(mixT_pool, len(WINDOWS))
                        r = slice(h % 2 * HD, (h % 2 + 1) * HD)
                        for t in range(TILES):
                            last = mm(ps[:, h, t * SEQ:(t + 1) * SEQ], qkT[r, h // 2, t * P:(t + 1) * P],
                                      qkT[r, 4 + h // 2, :])
                        last.then_inc(s_psum, 1)
                    for h in range(HEADS):
                        pe.wait_ge(p_done, TILES * (h + 1))
                        for k in range(TILES):
                            for t in range(TILES):
                                o = k * SEQ + t * P
                                last = nc.tensor.transpose(ps[:, h, o:o + P],
                                                           probs[:, h, t * SEQ + k * P:t * SEQ + (k + 1) * P],
                                                           ident[:, :])
                        last.then_inc(pT_psum, 1)
                    for j in range(HEADS // 2):
                        pe.wait_ge(pT_sb, 2 * j + 2)
                        if j < 2:
                            pe.wait_ge(pT_sb, 2 * j + 2)
                        for h in (2 * j, 2 * j + 1):
                            r = slice(h % 2 * HD, (h % 2 + 1) * HD)
                            for k in range(TILES):
                                v = proj[:, k, 2 * 512 + h * HD:2 * 512 + (h + 1) * HD]
                                last = mm(ps[r, j, 0:SEQ], v, probsT[:, h, k * SEQ:(k + 1) * SEQ],
                                          k == 0, k == TILES - 1)
                        last.then_inc(pv_psum, 1)
                    pe.wait_ge(mixT_attn, HEADS // 2)
                    pe.wait_ge(mixT_pool, len(WINDOWS))
                else:
                    pe.wait_ge(sgu_loaded, 48)
                    for t in range(TILES):
                        pe.wait_ge(vn_done, t + 1)
                        for k in range(2):
                            for g in range(4 * k, 4 * k + 4):
                                o = g % 4 * P
                                last = mm(ps[:, 4 + 2 * t + k, o:o + P], ws[:, g, :],
                                          vn[:, t, g * P:(g + 1) * P])
                            last.then_inc(sgu_psum, 1)
                    pe.wait_ge(gated_done, 4)
                    transpose_tokens(u_sb, 0, gT_psum)
                    pe.wait_ge(gT_sb, DC // 2)
                pe.wait_ge(wout_loaded, 16 * (l + 1))
                for t in range(TILES):
                    for k in range(2):
                        for c in range(DC):
                            last = mm(ps[:, 2 * t + k, :], mixT[:, c, t * P:(t + 1) * P],
                                      w_out[:, c, k * 512:(k + 1) * 512], c == 0, c == DC - 1)
                        last.then_inc(mix_psum, 1)

                pe.wait_ge(hn_done, 4 * l + 4)
                transpose_tokens(hn, 4, hT_psum)
                pe.wait_ge(hT_act, (2 * l + 2) * DC // 2)
                pe.wait_ge(hT_dve, (2 * l + 2) * DC // 2)
                for q in range(4):
                    pe.wait_ge(wbig_loaded[q], 16 * l + 32)
                for n in range(HALVES):
                    for c in range(DC):
                        last = mm(ps[:, n // 2, n % 2 * SEQ:(n % 2 + 1) * SEQ],
                                  w_q[:, c, n * P:(n + 1) * P], hTc[:, c, :], c == 0, c == DC - 1)
                    if n % 2:
                        last.then_inc(q_psum, 1)
                pe.wait_ge(qT_sb, (l + 1) * HALVES // 2)
                pe.wait_ge(subk_loaded, 16 * (l + 1))
                for t in range(TILES):
                    for n in range(HALVES):
                        o = n % 4 * P
                        last = mm(ps[:, 4 * t + n // 4, o:o + P], qT[:, n, t * P:(t + 1) * P], subk[:, n, :])
                        if n % 4 == 3:
                            last.then_inc(sc_psum, 1)

                pe.wait_ge(hi_done, l + 1)
                pe.wait_ge(lo_done, l + 1)
                pe.wait_ge(sc_sb, 8 * (l + 1))

                def down(b, s, first=False):
                    n = b + 2 * l * BLOCKS
                    pe.wait_ge(whi_done, n + 1)
                    pe.wait_ge(wlo_pool, b + l * BLOCKS + 1)
                    if not first:
                        pe.wait_ge(h_done, b + l * BLOCKS - RAW + 1)
                    for c in range(DC):
                        cs = slice(c * P, (c + 1) * P)
                        out = ps[:, s, 0:SEQ]
                        mm(out, whs[:, s, cs], hh[:, c, :], c == 0, False)
                        mm(out, whs[:, s, cs], hl[:, c, :], False, False)
                        last = mm(out, w_lo[:, s % WLO, cs], hh[:, c, :], False, c == DC - 1)
                    last.then_inc(w_used, 1)

                for b in range(RAW):
                    down(b, b, first=True)
                blocks(pe, down, RAW, IDS_AT)
                pe.wait_ge(idg_done, l + 1)
                for t in range(TILES):
                    nc.tensor.transpose(ps[:, 4, t * P:(t + 1) * P],
                                        hT[:, BEST_AT + t * P:BEST_AT + (t + 1) * P], ident[:, :])
                for t in range(TILES):
                    last = nc.tensor.transpose(ps[:, 4, SEQ + t * P:SEQ + (t + 1) * P], idf[:, t, :],
                                               ident[:, :])
                last.then_inc(idg_psum, 1)
                blocks(pe, down, IDS_AT, BLOCKS)

                with pe.Fori(0, TGROUPS // 4) as i:
                    for j in range(4):
                        g = i * 4 + j
                        pe.wait_ge(oh_built, g + 1 + l * TGROUPS)
                        for k in range(TOK):
                            out = ps[:, 4 + j, k * P:(k + 1) * P]
                            mm(out, oh2[:, j % 2, k, :], oh1h[:, j % 2, k, :], True, False)
                            last = mm(out, oh2[:, j % 2, k, :], oh1l[:, j % 2, k, :], False, True)
                        last.then_inc(g_mm, 1)

                def up(b, s, first=False, final=False):
                    pe.wait_ge(wlo_dve, b + l * BLOCKS + 1)
                    pe.wait_ge(ghlo_done, b + l * BLOCKS + 1)
                    for t in range(TILES):
                        ts = slice(t * P, (t + 1) * P)
                        for k in range(2):
                            out = ps[:, 2 * t + k, :]
                            ks = slice(k * 512, (k + 1) * 512)
                            mm(out, hh[:, s, ts], whs[:, s, ks], first, False)
                            mm(out, hh[:, s, ts], w_lo[:, s % WLO, ks], False, False)
                            last = mm(out, hl[:, s, ts], whs[:, s, ks], False, final)
                    last.then_inc(w_used, 1)

                for b in range(RAW):
                    up(b, b, first=b == 0)
                blocks(pe, up, RAW, BLOCKS - RAW)
                for b in range(BLOCKS - RAW, BLOCKS):
                    up(b, b % RAW, final=b == BLOCKS - 1)

        @block.vector
        def _(dve):
            steps = [0]
            norms = [0]

            def step(ins):
                steps[0] += 1
                return ins.then_inc(dve_step, 1)

            def settle():
                dve.wait_ge(dve_step, steps[0])

            def norm_scale():
                norms[0] += 1
                dve.wait_ge(sumsq_done, TILES * norms[0])
                nc.vector.tensor_scalar(meansq[:, :], sumsq[:, :], 1.0 / DM, EPS, ALU.mult,
                                        ALU.add).then_inc(ms_done, 1)
                dve.wait_ge(std_done, norms[0])
                dve.wait_ge(ms_done, norms[0])
                step(nc.vector.reciprocal(rinv[:, :], std[:, :]))
                settle()
                step(nc.vector.tensor_tensor(rtmp[:, :], rinv[:, :], rinv[:, :], ALU.mult))
                settle()
                step(nc.vector.tensor_tensor(rtmp[:, :], rtmp[:, :], meansq[:, :], ALU.mult))
                settle()
                step(nc.vector.tensor_scalar(rtmp[:, :], rtmp[:, :], -0.5, 1.5, ALU.mult, ALU.add))
                settle()
                step(nc.vector.tensor_tensor(rinv[:, :], rinv[:, :], rtmp[:, :], ALU.mult))
                settle()

            def norm_tokens():
                norm_scale()
                for t in range(TILES):
                    nc.vector.tensor_scalar(hn[:, t, :], xs[:, t, :], rinv[:, t:t + 1], None,
                                            ALU.mult).then_inc(hn_done, 1)

            def evacuate_hT(k, bank):
                for c in range(DC // 2, DC):
                    dve.wait_ge(hT_psum, k * DC // 2 + c // 2 + 1)
                    nc.vector.tensor_scalar(hTc[:, c, :], ps[:, bank + c // 2, c % 2 * SEQ:(c % 2 + 1) * SEQ],
                                            gam[:, k, c:c + 1], None, ALU.mult).then_inc(hT_dve, 1)

            def add_residual(done, base):
                for i in range(4):
                    t, k = divmod(i, 2)
                    dve.wait_ge(done, base(i))
                    part = xs[:, t, k * 512:(k + 1) * 512]
                    nc.vector.tensor_tensor(part, part, ps[:, i, :], ALU.add).then_inc(x_ready, 1)

            dve.wait_ge(x_loaded, 16)
            for l in range(LAYERS):
                if l:
                    dve.wait_ge(x_ready, 8 * l)
                norm_tokens()
                if l == 0:
                    dve.wait_ge(consts_loaded, 32)
                evacuate_hT(2 * l, 0)
                if l == 0:
                    dve.wait_ge(tabs_loaded, 112)
                    for t in range(TILES):
                        dve.wait_ge(proj_sb, NB * t + 2)
                        qk = proj[:, t, 0:2 * 512].rearrange("p (h d) -> p h d", d=HD)
                        t1, t2 = qk[:, :, 0:ROT], qk[:, :, ROT:2 * ROT]
                        cos = tab[:, 0, t, :].unsqueeze(1).to_broadcast([P, 2 * HEADS, ROT])
                        sin = tab[:, 1, t, :].unsqueeze(1).to_broadcast([P, 2 * HEADS, ROT])
                        if t:
                            dve.wait_ge(rot_done, t)
                        step(nc.vector.tensor_tensor(rot[:, 0], t1, cos, ALU.mult))
                        step(nc.vector.tensor_tensor(rot[:, 1], t2, sin, ALU.mult))
                        step(nc.vector.tensor_tensor(rot[:, 2], t2, cos, ALU.mult))
                        step(nc.vector.tensor_tensor(rot[:, 3], t1, sin, ALU.mult))
                        settle()
                        step(nc.vector.tensor_tensor(t1, rot[:, 0], rot[:, 1], ALU.subtract))
                        settle()
                        nc.vector.tensor_tensor(t2, rot[:, 2], rot[:, 3], ALU.add).then_inc(rot_done, 1)
                    for i in range(DC // 2):
                        dve.wait_ge(qkT_psum, i + 1)
                        nc.vector.tensor_copy(qkT[:, 2 * i:2 * i + 2, :],
                                              ps[:, i, :].rearrange("p (c t) -> p c t", t=SEQ)
                                              ).then_inc(qkT_sb, 1)

                    def weigh(h):
                        dve.wait_ge(s_psum, h + 1)
                        step(nc.vector.scalar_tensor_tensor(probs[:, h, :], ps[:, h, :], HD ** -0.5,
                                                            lncount, ALU.mult, ALU.add))
                        settle()
                        step(nc.vector.reduce_max(rowmax[:, h, :], probs[:, h, :].rearrange(
                            "p (t k) -> p t k", k=SEQ), AX.X))
                        settle()
                        nc.vector.tensor_scalar(rowmax[:, h, :], rowmax[:, h, :], -1.0, None,
                                                ALU.mult).then_inc(nmax_done, 1)

                    def normalise(h):
                        dve.wait_ge(exp_done, TILES * (h + 1))
                        step(nc.vector.reciprocal(rowinv[:, h, :], rowsum[:, h, :]))
                        settle()
                        for t in range(TILES):
                            p = probs[:, h, t * SEQ:(t + 1) * SEQ]
                            nc.vector.tensor_scalar(p, p, rowinv[:, h, t:t + 1], None,
                                                    ALU.mult).then_inc(p_done, 1)

                    for h in range(HEADS):
                        weigh(h)
                        if h:
                            normalise(h - 1)
                    normalise(HEADS - 1)
                else:
                    norm_scale()
                    dve.wait_ge(sgu_loaded, 48)
                    for t in range(TILES):
                        nc.vector.scalar_tensor_tensor(vn[:, t, :], v_sb[:, t, :], rinv[:, t:t + 1], cnorm,
                                                       ALU.mult, ALU.mult).then_inc(vn_done, 1)
                    for i in range(4):
                        t, k = divmod(i, 2)
                        dve.wait_ge(sgu_psum, i + 1)
                        for g in range(4 * k, 4 * k + 4):
                            part = u_sb[:, t, g * P:(g + 1) * P]
                            o = g % 4 * P
                            last = nc.vector.scalar_tensor_tensor(part, ps[:, 4 + i, o:o + P], bs[:, g:g + 1],
                                                                  part, ALU.add, ALU.mult)
                            if g % 4 < 3:
                                step(last)
                        last.then_inc(gated_done, 1)
                add_residual(mix_psum, lambda i: 4 * l + i + 1)

                dve.wait_ge(x_ready, 8 * l + 4)
                norm_tokens()
                evacuate_hT(2 * l + 1, 4)
                dve.wait_ge(hi_done, l + 1)
                dve.wait_ge(hT_dve, (2 * l + 2) * DC // 2)
                nc.vector.tensor_tensor(hT_lo[:, :], hT[:, :], hT_hi[:, :].bitcast(F32),
                                        ALU.subtract).then_inc(lo_done, 1)

                def top16(rows):
                    for r in range(0, len(rows), 4):
                        some = rows[r:r + 4]
                        for half in (slice(0, 8), slice(8, 16)):
                            settle()
                            for vals, top, pos in some:
                                step(nc.vector.max(top[:, half], vals))
                            settle()
                            for vals, top, pos in some:
                                step(nc.vector.max_index(pos[:, half], top[:, half], vals))
                            if half.start == 0:
                                settle()
                                for vals, top, pos in some:
                                    step(nc.vector.match_replace(vals, top[:, half], vals, LOWEST))

                for t in range(TILES):
                    dve.wait_ge(sc_sb, 8 * l + 4 * (t + 1))
                    top16([(scores[:, t, n * KEYS:(n + 1) * KEYS], sv[:, t, n, :], si[:, t, n, :])
                           for n in range(HALVES)])
                    settle()
                    step(nc.vector.tensor_copy(sif[:, t].rearrange("p h i k -> p (h i) k"), si[:, t]))
                    settle()
                    step(nc.vector.tensor_scalar(sif[:, t, :, 0, :], sif[:, t, :, 0, :], float(KEYS), None,
                                                 ALU.mult))
                    settle()
                    svt = sv[:, t].rearrange("p (h i) k -> p h i k", i=2)
                    o = 0
                    for a0, a1, nb in SEGS:
                        na = a1 - a0
                        for dst, src in ((cand, svt), (pay, sif[:, t])):
                            d = dst[:, :, o:o + na * nb].rearrange("p h (a b) -> p h a b", b=nb)
                            f = src[:, :, 0, a0:a1].unsqueeze(3).to_broadcast([P, RH, na, nb])
                            s = src[:, :, 1, 0:nb].unsqueeze(2).to_broadcast([P, RH, na, nb])
                            step(nc.vector.tensor_tensor(d, f, s, ALU.add))
                        o += na * nb
                    top16([(cand[:, h, :], best[:, t, h, :], ci[:, t, h, :]) for h in range(RH)])
                    settle()
                    step(nc.vector.tensor_copy(cif[:, t], ci[:, t].rearrange("p h k -> p (h k)")))
                    settle()
                    for h in range(0, RH, 2):
                        n = 2 * TOPK
                        step(nc.vector.tensor_tensor(
                            eq, iotac[:, :].unsqueeze(1).to_broadcast([P, n, CAND]),
                            cif[:, t, h * TOPK:h * TOPK + n].unsqueeze(2).to_broadcast([P, n, CAND]),
                            ALU.is_equal))
                        settle()
                        e4 = eq.rearrange("p (h k) c -> p h k c", k=TOPK)
                        step(nc.vector.tensor_tensor(
                            e4, e4, pay[:, h:h + 2, :].unsqueeze(2).to_broadcast([P, 2, TOPK, CAND]),
                            ALU.mult))
                        settle()
                        step(nc.vector.reduce_sum(idf[:, t, h * TOPK:h * TOPK + n], eq, AX.X))
                        settle()
                b3 = best.rearrange("p t h k -> p (t h) k")
                gs = gsum[:, :, :].rearrange("p a h -> p (a h)")
                top, tot = gs[:, 0:TILES * RH], gs[:, TILES * RH:2 * TILES * RH]
                wide = [P, TILES * RH, TOPK]
                step(nc.vector.tensor_copy(top, b3[:, :, 0]))
                settle()
                nc.vector.tensor_tensor(b3, b3, top.unsqueeze(2).to_broadcast(wide),
                                        ALU.subtract).then_inc(best_done, 1)
                dve.wait_ge(gexp_done, l + 1)
                step(nc.vector.reduce_sum(tot, b3, AX.X))
                settle()
                step(nc.vector.reciprocal(tot, tot))
                settle()
                nc.vector.tensor_tensor(b3, b3, tot.unsqueeze(2).to_broadcast(wide),
                                        ALU.mult).then_inc(idg_done, 1)
                dve.wait_ge(idg_psum, l + 1)
                step(nc.vector.tensor_copy(gT, ps[:, 4, 0:SEQ]))
                step(nc.vector.tensor_copy(idi, ps[:, 4, SEQ:2 * SEQ]))
                settle()
                step(nc.vector.tensor_copy(g_hi[:, :], gT))
                step(nc.vector.tensor_scalar(idk, idi, 7, None, ALU.arith_shift_right))
                settle()
                step(nc.vector.tensor_tensor(g_lo, gT, g_hi[:, :].bitcast(F32), ALU.subtract))
                step(nc.vector.tensor_copy(i1T, idk))
                step(nc.vector.tensor_scalar(idi, idi, KEYS - 1, None, ALU.bitwise_and))
                settle()
                step(nc.vector.tensor_copy(i2T, idi))
                settle()

                def build(g, s, first=False):
                    if not first:
                        dve.wait_ge(g_mm, g - 1 + l * TGROUPS)
                    for k in range(TOK):
                        t = bass.ds(g * TOK + k, 1)
                        nc.vector.tensor_scalar(oh2[:, s, k, :], iota[:, :], i2T[:, t], None, ALU.is_equal)
                        nc.vector.tensor_scalar(oh1h[:, s, k, :], iota[:, :], i1T[:, t], gT[:, t],
                                                ALU.is_equal, ALU.mult)
                        last = nc.vector.tensor_scalar(oh1l[:, s, k, :], iota[:, :], i1T[:, t], g_lo[:, t],
                                                       ALU.is_equal, ALU.mult)
                    last.then_inc(oh_built, 1)

                def gate(g, s):
                    dve.wait_ge(g_mm, g + 1 + l * TGROUPS)
                    part = H[:, :, bass.ds(g * TOK, TOK)]
                    nc.vector.tensor_tensor(part, part, ps[:, 4 + s, :].rearrange("p (t i) -> p i t", t=TOK),
                                            ALU.mult).then_inc(gmul_done, 1)

                dve.wait_ge(w_used, (2 * l + 1) * BLOCKS)
                dve.wait_ge(h_done, (l + 1) * BLOCKS)
                build(0, 0, first=True)
                build(1, 1, first=True)
                gate(0, 0)
                for g in (2, 3, 4):
                    build(g, g % 2)
                    gate(g - 1, g - 1)
                with dve.Fori(1, TGROUPS // 4 - 1) as i:
                    for j in range(4):
                        build(i * 4 + j + 1, (j + 1) % 2)
                        gate(i * 4 + j, j)
                for g in range(TGROUPS - 4, TGROUPS):
                    if g + 1 < TGROUPS:
                        build(g + 1, (g + 1) % 2)
                    gate(g, g % 4)

                def up(b, s):
                    n = b + (2 * l + 1) * BLOCKS
                    dve.wait_ge(whi_done, n + 1)
                    dve.wait_ge(w_used, n - WLO + 1)
                    nc.vector.tensor_tensor(w_lo[:, s % WLO, :], raw[:, s, :], whs[:, s].bitcast(F32),
                                            ALU.subtract).then_inc(wlo_dve, 1)
                    dve.wait_ge(ghhi_done, b + l * BLOCKS + 1)
                    nc.vector.tensor_tensor(hl[:, s, :], arena[:, bass.ds(b * SEQ, SEQ)],
                                            hh[:, s, :].bitcast(F32), ALU.subtract).then_inc(ghlo_done, 1)

                blocks(dve, up, 0, BLOCKS)
                add_residual(w_used, lambda i: (2 * l + 2) * BLOCKS)
            dve.wait_ge(x_ready, 8 * LAYERS)
            norm_scale()
            dve.wait_ge(gfin_loaded, 16)
            for t in range(TILES):
                nc.vector.scalar_tensor_tensor(hn[:, t, :], xs[:, t, :], rinv[:, t:t + 1], cnorm, ALU.mult,
                                               ALU.mult).then_inc(hn_done, 1)


def shape_tables():
    f = np.float32
    pos = np.arange(SEQ, dtype=f)
    inv = (f(500000.0) ** (-np.arange(0, 2 * ROT, 2, dtype=f) / f(2 * ROT))).astype(f)
    ang = (pos[:, None] * inv[None, :]).astype(f)
    tab = np.stack([np.cos(ang), np.sin(ang)]).astype(f).reshape(2, TILES, P, ROT).transpose(2, 0, 1, 3)
    rel = np.abs(np.arange(SEQ)[:, None] - np.arange(SEQ)[None, :])
    count = sum(((rel % dil == 0) & (rel <= window // 2)).astype(np.float64) for window, dil in PATTERNS)
    lncount = np.where(count > 0, np.log(np.maximum(count, 1)), -1e30).astype(f)
    lncount = lncount.reshape(TILES, P, SEQ).transpose(1, 0, 2).reshape(P, TILES * SEQ)
    poolm = np.zeros((SEQ, len(WINDOWS), SEQ), f)
    for g, win in enumerate(WINDOWS):
        for t in range(SEQ):
            lo, hi = max(t - win // 2, 0), min(t + win - win // 2, SEQ)
            poolm[lo:hi, g, t] = 1.0 / (hi - lo)
            poolm[t, g, t] -= 1.0
    poolm = poolm.reshape(TILES, P, len(WINDOWS), SEQ).transpose(1, 0, 2, 3)
    ones = np.ones((P, 1), f)
    return {"tab": tab, "lncount": lncount, "poolm": poolm, "ident": np.eye(P, dtype=f),
            "iota": ones * np.arange(P, dtype=f), "iotac": ones * np.arange(CAND, dtype=f)}


def kernel(**inputs):
    import numpy as _np
    import concourse.bacc as _bacc
    from concourse import mybir as _mybir
    from concourse.bass_utils import run_bass_kernel_spmd as _run

    a = {k: _np.asarray(v) for k, v in inputs.items()}

    def chunks(w):
        return w.reshape(w.shape[0], DC, P, -1).transpose(0, 2, 1, 3)

    gammas = _np.stack([a["norm_mix"], a["norm_ffn"]], axis=1).reshape(2 * LAYERS, DC, P)
    arrays = {
        "x": a["x"].reshape(TILES, P, DM).transpose(1, 0, 2),
        "gam": gammas.transpose(2, 0, 1),
        "gfin": _np.broadcast_to(a["norm_final"], (P, DM)),
        **shape_tables(),
        "poolw": a["pool_w"][0].transpose(1, 0, 2),
        "pscale": a["pool_scale"].reshape(len(WINDOWS), P).transpose(1, 0),
        "w_in": chunks(_np.concatenate([a["ab_w_in"], a["c_w_in"]])),
        "w_out": chunks(_np.concatenate([a["ab_w_out"], a["c_w_out"]])),
        "ws": a["c_w_s"][0].transpose(2, 0, 1),
        "bs": a["c_b_s"][0].transpose(1, 0),
        "cnorm": _np.broadcast_to(a["c_norm"].reshape(DM), (P, DM)),
        "wq": chunks(a["peer_w_q"]),
        "subk": a["peer_sub_keys"].reshape(LAYERS, HALVES, KEYS, P).transpose(0, 3, 1, 2),
        "wd": a["peer_w_down"].reshape(LAYERS, BLOCKS, KEYS, DC, P).transpose(0, 1, 4, 3, 2).reshape(
            LAYERS, BLOCKS, P, DM),
        "wu": a["peer_w_up"].reshape(LAYERS, BLOCKS, KEYS, DM),
    }
    order = ["x", "gam", "gfin", "tab", "ident", "iota", "iotac", "lncount", "poolm", "poolw", "pscale",
             "w_in", "w_out", "ws", "bs", "cnorm", "wq", "subk", "wd", "wu"]
    nc = _bacc.Bacc("TRN2", target_bir_lowering=False, num_devices=1)
    feeds, args = {}, []
    for name in order:
        arr = _np.ascontiguousarray(arrays[name])
        feeds[f"in_{name}"] = arr
        args.append(nc.dram_tensor(f"in_{name}", arr.shape, _mybir.dt.from_np(arr.dtype),
                                   kind="ExternalInput").ap())
    out = nc.dram_tensor("out", (P, TILES, DM), _mybir.dt.float32, kind="ExternalOutput").ap()
    build_trunk(nc, *args, out)
    r = _run(nc, [feeds], core_ids=[0])
    return r.results[0]["out"].transpose(1, 0, 2).reshape(1, SEQ, DM)
```

```python
from contextlib import ExitStack

import numpy as np

import concourse.bass as bass
from concourse import mybir

F32 = mybir.dt.float32
F32R = mybir.dt.float32r
I32 = mybir.dt.int32
U32 = mybir.dt.uint32
ALU = mybir.AluOpType
ACT = mybir.ActivationFunctionType
AX = mybir.AxisListType

P = 128
LAYERS = 2
SEQ = 256
TILES = SEQ // P
DM = 1024
DC = DM // P
PROJ = 2048
NB = PROJ // 512
EPS = 1e-6

HEADS = 8
HD = 64
ROT = HD // 8
WINDOWS = (2, 4, 8, 16)
PATTERNS = ((128, 1), (512, 4), (2048, 16))
GROUPS = 8

RH = 8
HALVES = 2 * RH
KEYS = 128
TOPK = 16
SEGS = ((0, 1, 16), (1, 2, 8), (2, 4, 5), (4, 8, 3), (8, 16, 1))
CAND = sum((a1 - a0) * nb for a0, a1, nb in SEGS)
LOWEST = -3.0e38

BLOCKS = KEYS
RAW = 4
WHI = 4
WLO = 2
GHS = 4
TOK = 4
TGROUPS = SEQ // TOK
IN_BLOCKS, OUT_BLOCKS, Q_BLOCKS = 16, 8, 16
MIX_BLOCKS = IN_BLOCKS + OUT_BLOCKS + Q_BLOCKS
Q_FROM = IN_BLOCKS + OUT_BLOCKS
UP_FROM = MIX_BLOCKS + BLOCKS
LAYER = UP_FROM + BLOCKS
EXP_AT = 36
IDS_AT = 40
G_FROM = 48
G_TO = G_FROM + TGROUPS

SUBK_AT = 0
WS_AT = 2048
CN_AT = 3072
BS_AT = 4096
POOLM_AT = 4608
POOLED_AT = 6656
POOLW_AT = 7680
LN_AT = 8192
ROT_AT = 8704
QT_AT = 9216
PROJ_AT = 16384
QKT_AT = 20480
VN_AT = 20480
PR_AT = 22528
PT_AT = 26624
HN_AT = 30720
EQ_AT = 24448
SV_AT = 26176
SI_AT = 26688
SIF_AT = 27200
CD_AT = 27712
PAY_AT = 28144
SC_AT = 28672
SMALL_FREE_AT = 20
assert EQ_AT + 32 * CAND <= SV_AT and PAY_AT + RH * CAND <= SC_AT and G_FROM * SEQ <= EQ_AT
assert BS_AT + GROUPS <= SMALL_FREE_AT * SEQ
BEST_AT, CIF_AT, IDF_AT, CI_AT = 1024, 1280, 1536, 1792


def build_trunk(nc, x_d, gam_d, gfin_d, tab_d, ident_d, iota_d, iotac_d, lncount_d, poolm_d, poolw_d,
                pscale_d, wm_d, ws_d, bs_d, cnorm_d, subk_d, wd_d, wu_d, out_d):
    ctx = ExitStack()
    with ctx:
        def sb(name, shape, dt):
            return ctx.enter_context(nc.sbuf_tensor(name, shape, dt))

        def sem(name):
            return ctx.enter_context(nc.semaphore(name))

        arena = sb("arena", [P, BLOCKS * SEQ], F32)
        xs = sb("xs", [P, TILES, DM], F32)
        ret = sb("ret", [P, DC * SEQ], F32)
        oh_buf = sb("oh_buf", [P, 2 * TOK * P], F32)
        hT_hi = sb("hT_hi", [P, DC * SEQ], F32R)
        hT_lo = sb("hT_lo", [P, DC * SEQ], F32R)
        raw = sb("raw", [P, RAW, DM], F32)
        w_hi = sb("w_hi", [P, WHI * DM], F32R)
        w_lo = sb("w_lo", [P, WLO, DM], F32R)
        ident = sb("ident", [P, P], F32)
        iota = sb("iota", [P, P], F32)
        iotac = sb("iotac", [P, CAND], F32)
        gam = sb("gam", [P, 2 * LAYERS, DC], F32)
        tab = sb("tab", [P, 2, TILES, ROT], F32)
        pscale = sb("pscale", [P, len(WINDOWS)], F32)
        sumsq = sb("sumsq", [P, TILES], F32)
        meansq = sb("meansq", [P, TILES], F32)
        std = sb("std", [P, TILES], F32)
        rinv = sb("rinv", [P, TILES], F32)
        rtmp = sb("rtmp", [P, TILES], F32)
        rowmax = sb("rowmax", [P, HEADS, TILES], F32)
        rowsum = sb("rowsum", [P, HEADS, TILES], F32)
        rowinv = sb("rowinv", [P, HEADS, TILES], F32)
        gsum = sb("gsum", [P, 2 * TILES, RH], F32)
        ps = ctx.enter_context(nc.psum_tensor("ps", [P, 8, 512], F32))

        def at(start, *dims):
            size = int(np.prod(dims))
            v = arena[:, start:start + size]
            if len(dims) == 1:
                return v
            names = "abcd"[:len(dims)]
            return v.rearrange(f"p ({' '.join(names)}) -> p {' '.join(names)}",
                               **{k: d for k, d in zip(names, dims)})

        H = arena[:, :].rearrange("p (i t) -> p i t", t=SEQ)
        rot = at(ROT_AT, 4, 2 * HEADS, ROT)
        proj = at(PROJ_AT, TILES, PROJ)
        u_sb = at(PROJ_AT, TILES, DM)
        v_sb = at(PROJ_AT + TILES * DM, TILES, DM)
        vn = at(VN_AT, TILES, DM)
        qkT = at(QKT_AT, DC, SEQ)
        probs = at(PR_AT, HEADS, TILES * SEQ)
        probsT = at(PT_AT, HEADS, TILES * SEQ)
        poolm = at(POOLM_AT, TILES, len(WINDOWS), SEQ)
        pooledT = at(POOLED_AT, len(WINDOWS), SEQ)
        ws = at(WS_AT, GROUPS, P)
        cnorm = at(CN_AT, DM)
        bs = at(BS_AT, GROUPS)
        hn = at(HN_AT, TILES, DM)
        qT = at(QT_AT, HALVES, SEQ)
        subk = at(SUBK_AT, HALVES, KEYS)
        scores = at(SC_AT, TILES, HALVES * KEYS)
        sv = at(SV_AT, TILES, HALVES, TOPK)
        si = arena[:, SI_AT:SI_AT + TILES * HALVES * TOPK].bitcast(U32).rearrange(
            "p (a b c) -> p a b c", a=TILES, b=HALVES)
        sif = at(SIF_AT, TILES, RH, 2, TOPK)
        cand = at(CD_AT, RH, CAND)
        pay = at(PAY_AT, RH, CAND)
        eq = at(EQ_AT, 2 * TOPK, CAND)
        lncount = at(LN_AT, TILES * SEQ)
        poolw = at(POOLW_AT, len(WINDOWS), P)

        i1T, i2T, gT = ret[:, 0:SEQ], ret[:, SEQ:2 * SEQ], ret[:, 2 * SEQ:3 * SEQ]
        best = ret[:, BEST_AT:BEST_AT + TILES * P].rearrange("p (t h k) -> p t h k", t=TILES, h=RH)
        cif = ret[:, CIF_AT:CIF_AT + TILES * P].rearrange("p (t n) -> p t n", t=TILES)
        idf = ret[:, IDF_AT:IDF_AT + TILES * P].rearrange("p (t n) -> p t n", t=TILES)
        ci = ret[:, CI_AT:CI_AT + TILES * P].bitcast(U32).rearrange("p (t h k) -> p t h k", t=TILES, h=RH)
        idi = ret[:, CIF_AT:CIF_AT + SEQ].bitcast(I32)
        idk = ret[:, CI_AT:CI_AT + SEQ].bitcast(I32)

        hh = hT_hi[:, :].rearrange("p (c t) -> p c t", t=SEQ)
        hl = hT_lo[:, :].rearrange("p (c t) -> p c t", t=SEQ)
        whs = w_hi[:, :].rearrange("p (s n) -> p s n", s=WHI)
        def ring(v):
            return v.rearrange("p (s t i) -> p s t i", s=2, t=TOK)

        oh2 = ring(ret[:, BEST_AT:BEST_AT + 2 * TOK * P])
        oh1g = ring(oh_buf[:, :])

        x_loaded, consts_loaded, tabs_loaded = sem("x_loaded"), sem("consts_loaded"), sem("tabs_loaded")
        subk_loaded = sem("subk_loaded")
        sgu_loaded, gfin_loaded = sem("sgu_loaded"), sem("gfin_loaded")
        raw_full = [sem(f"raw_full{s}") for s in range(RAW)]
        out_stored = sem("out_stored")
        sumsq_done, ms_done, std_done = sem("sumsq_done"), sem("ms_done"), sem("std_done")
        hn_done, hT_psum = sem("hn_done"), sem("hT_psum")
        hh_done, hl_done = sem("hh_done"), sem("hl_done")
        x_ready = sem("x_ready")
        proj_sb = sem("proj_sb")
        pool_psum, pooled_sb, poolmix_psum = sem("pool_psum"), sem("pooled_sb"), sem("poolmix_psum")
        rot_done, qkT_psum, qkT_sb = sem("rot_done"), sem("qkT_psum"), sem("qkT_sb")
        s_psum, nmax_done, exp_done, p_done = sem("s_psum"), sem("nmax_done"), sem("exp_done"), sem("p_done")
        pT_psum, pT_sb, pv_psum = sem("pT_psum"), sem("pT_sb"), sem("pv_psum")
        vn_done, sgu_psum, gated_done = sem("vn_done"), sem("sgu_psum"), sem("gated_done")
        gT_psum = sem("gT_psum")
        qT_sb, sc_psum, sc_sb = sem("qT_sb"), sem("sc_psum"), sem("sc_sb")
        best_done, gexp_done, idg_done, idg_psum = (
            sem("best_done"), sem("gexp_done"), sem("idg_done"), sem("idg_psum"))
        whi_done, wlo_pool, wlo_dve, w_used = sem("whi_done"), sem("wlo_pool"), sem("wlo_dve"), sem("w_used")
        h_done, h_psum, hmul_done = sem("h_done"), sem("h_psum"), sem("hmul_done")
        ghhi_done, ghlo_done = sem("ghhi_done"), sem("ghlo_done")
        oh_built, g_mm, gmul_done = sem("oh_built"), sem("g_mm"), sem("gmul_done")
        dve_step = sem("dve_step")
        iota3 = iota[:, :].unsqueeze(1).to_broadcast([P, TOK, P])

        def blocks(eng, body, first, last):
            with eng.Fori(first // RAW, last // RAW) as i:
                for j in range(RAW):
                    body(i * RAW + j, j)

        block = ctx.enter_context(nc.Block())


        @block.sync
        def _(sp):
            sp.dma_start(xs[:, :, :], x_d).then_inc(x_loaded, 16)
            sp.dma_start(ident[:, :], ident_d).then_inc(consts_loaded, 16)
            sp.dma_start(gam[:, :, :], gam_d).then_inc(consts_loaded, 16)
            for l in range(LAYERS):
                def load(src, row, used, count, s):
                    sp.wait_ge(used, count)
                    sp.dma_start(raw[:, s, :], src[l, bass.ds(row, 1)].rearrange("b p n -> p (b n)")
                                 ).then_inc(raw_full[s], 16)

                for s in range(RAW):
                    if l:
                        sp.wait_ge(wlo_dve, l * BLOCKS - RAW + 1 + s)
                    sp.dma_start(raw[:, s, :], wm_d[l, s]).then_inc(raw_full[s], 16)
                if l == 0:
                    sp.dma_start(tab[:, :, :, :], tab_d).then_inc(tabs_loaded, 16)
                    sp.dma_start(pscale[:, :], pscale_d).then_inc(tabs_loaded, 16)
                    sp.dma_start(iota[:, :], iota_d).then_inc(tabs_loaded, 16)
                    sp.dma_start(iotac[:, :], iotac_d).then_inc(tabs_loaded, 16)
                    sp.dma_start(poolm, poolm_d).then_inc(tabs_loaded, 16)
                    sp.dma_start(poolw, poolw_d).then_inc(tabs_loaded, 16)
                    sp.dma_start(lncount, lncount_d).then_inc(tabs_loaded, 16)
                    sp.dma_start(subk, subk_d[l]).then_inc(subk_loaded, 16)
                blocks(sp, lambda b, s: load(wm_d, b, wlo_pool, l * UP_FROM + b - RAW + 1, s),
                       RAW, MIX_BLOCKS)
                blocks(sp, lambda b, s: load(wd_d, b, wlo_pool, l * UP_FROM + MIX_BLOCKS + b - RAW + 1, s),
                       0, BLOCKS)
                for s in range(RAW):
                    sp.wait_ge(wlo_pool, (l + 1) * UP_FROM - RAW + 1 + s)
                    sp.dma_start(raw[:, s, :], wu_d[l, s]).then_inc(raw_full[s], 16)

                def load_up(b, s):
                    load(wu_d, b, wlo_dve, l * BLOCKS + b - RAW + 1, s)

                blocks(sp, load_up, RAW, 2 * SMALL_FREE_AT)
                sp.wait_ge(ghlo_done, l * BLOCKS + SMALL_FREE_AT)
                if l == 0:
                    sp.dma_start(ws, ws_d).then_inc(sgu_loaded, 16)
                    sp.dma_start(bs, bs_d).then_inc(sgu_loaded, 16)
                    sp.dma_start(cnorm, cnorm_d).then_inc(sgu_loaded, 16)
                    sp.dma_start(subk, subk_d[1]).then_inc(subk_loaded, 16)
                else:
                    sp.dma_start(cnorm, gfin_d).then_inc(gfin_loaded, 16)
                blocks(sp, load_up, 2 * SMALL_FREE_AT, BLOCKS)
            for t in range(TILES):
                sp.wait_ge(hn_done, 4 * LAYERS + t + 1)
                sp.dma_start(out_d[:, t, :], hn[:, t, :]).then_inc(out_stored, 16)
            sp.wait_ge(out_stored, 16 * TILES)

        @block.gpsimd
        def _(pool):
            for l in range(LAYERS):
                def low_part(b, s, first=False):
                    n = b + l * LAYER
                    pool.wait_ge(whi_done, n + 1)
                    if not first:
                        pool.wait_ge(w_used, n - WLO + 1)
                    nc.gpsimd.tensor_tensor(w_lo[:, s % WLO, :], raw[:, s, :],
                                            whs[:, s].bitcast(F32), ALU.subtract).then_inc(wlo_pool, 1)

                for b in range(RAW):
                    low_part(b, b, first=l == 0 and b < WLO)
                blocks(pool, low_part, RAW, UP_FROM)

        @block.scalar
        def _(act):
            norms = [0]

            def norm_stats(src, junk):
                norms[0] += 1
                for t in range(TILES):
                    nc.scalar.activation(junk[:, t, :], src[:, t, :], ACT.Square,
                                         accum_out=sumsq[:, t:t + 1]).then_inc(sumsq_done, 1)
                act.wait_ge(ms_done, norms[0])
                nc.scalar.activation(std[:, :], meansq[:, :], ACT.Sqrt).then_inc(std_done, 1)

            def high_part(n, s, first=False):
                act.wait_ge(raw_full[s], (n - s) * (16 // RAW) + 16)
                if not first:
                    act.wait_ge(w_used, n - WHI + 1)
                nc.scalar.activation(whs[:, s], raw[:, s, :], ACT.Copy).then_inc(whi_done, 1)

            def high_parts(first, last):
                blocks(act, high_part, first, last)

            def split_chunks(ready, base, bank, scale):
                for c in range(DC):
                    act.wait_ge(ready, base + c // 2 + 1)
                    src = ps[:, bank + c // 2, c % 2 * SEQ:(c % 2 + 1) * SEQ]
                    nc.scalar.activation(hh[:, c, :], src, ACT.Copy, scale=scale(c)).then_inc(hh_done, 1)

            for s in range(RAW):
                high_part(s, s, first=True)
            act.wait_ge(x_loaded, 16)
            for l in range(LAYERS):
                if l:
                    act.wait_ge(x_ready, 8 * l)
                norm_stats(xs, hn)
                if l == 0:
                    act.wait_ge(consts_loaded, 32)
                split_chunks(hT_psum, 8 * l, 0, lambda c: gam[:, 2 * l, c:c + 1])

                def take_projection(f):
                    act.wait_ge(w_used, l * LAYER + (f + 1) * DC)
                    for i in range(4):
                        t, k = divmod(i, 2)
                        src = ps[:, 4 * (1 - f) + i, :]
                        if l == 0:
                            o = f * DM + k * 512
                            nc.scalar.activation(proj[:, t, o:o + 512], src, ACT.Copy).then_inc(proj_sb, 1)
                        else:
                            dst = (v_sb if f else u_sb)[:, t, k * 512:(k + 1) * 512]
                            nc.scalar.activation(dst, src, ACT.Gelu_apprx_tanh).then_inc(proj_sb, 1)

                high_parts(l * LAYER + RAW, l * LAYER + 12)
                take_projection(0)
                high_parts(l * LAYER + 12, l * LAYER + 20)
                take_projection(1)
                if l == 0:
                    for g in range(len(WINDOWS)):
                        act.wait_ge(pool_psum, g + 1)
                        nc.scalar.activation(pooledT[:, g, :], ps[:, 4 + g, 0:SEQ],
                                             ACT.Copy).then_inc(pooled_sb, 1)
                    act.wait_ge(tabs_loaded, 112)
                    for g in range(len(WINDOWS)):
                        act.wait_ge(poolmix_psum, g + 1)
                        nc.scalar.activation(hh[:, 4 + g, :], ps[:, 4 + g, SEQ:2 * SEQ], ACT.Copy,
                                             scale=pscale[:, g:g + 1]).then_inc(hh_done, 1)

                    def take_probsT(h):
                        act.wait_ge(pT_psum, h + 1)
                        nc.scalar.activation(probsT[:, h, :], ps[:, h, :], ACT.Copy).then_inc(pT_sb, 1)

                    for h in range(HEADS):
                        act.wait_ge(nmax_done, h + 1)
                        for t in range(TILES):
                            p = probs[:, h, t * SEQ:(t + 1) * SEQ]
                            nc.scalar.activation(p, p, ACT.Exp, bias=rowmax[:, h, t:t + 1],
                                                 accum_out=rowsum[:, h, t:t + 1]).then_inc(exp_done, 1)
                        if h >= 2:
                            take_probsT(h - 2)
                    take_probsT(HEADS - 2)
                    take_probsT(HEADS - 1)
                    for j in range(HEADS // 2):
                        act.wait_ge(pv_psum, j + 1)
                        nc.scalar.activation(hh[:, j, :], ps[:, j, 0:SEQ], ACT.Copy).then_inc(hh_done, 1)
                else:
                    act.wait_ge(proj_sb, 8 * LAYERS)
                    norm_stats(v_sb, vn)
                    split_chunks(gT_psum, 0, 0, lambda c: 1.0)

                high_parts(l * LAYER + 20, l * LAYER + Q_FROM + 4)
                act.wait_ge(x_ready, 8 * l + 4)
                norm_stats(xs, hn)
                split_chunks(hT_psum, 8 * l + 4, 4, lambda c: gam[:, 2 * l + 1, c:c + 1])

                def take_queries(f):
                    act.wait_ge(w_used, l * LAYER + Q_FROM + (f + 1) * DC)
                    for i in range(4 * f, 4 * f + 4):
                        nc.scalar.activation(qT[:, 2 * i:2 * i + 2, :],
                                             ps[:, i, :].rearrange("p (c t) -> p c t", t=SEQ),
                                             ACT.Copy).then_inc(qT_sb, 1)

                high_parts(l * LAYER + Q_FROM + 4, l * LAYER + Q_FROM + 12)
                take_queries(0)
                high_parts(l * LAYER + Q_FROM + 12, l * LAYER + MIX_BLOCKS + RAW)
                take_queries(1)
                for i in range(8):
                    act.wait_ge(sc_psum, 8 * l + i + 1)
                    nc.scalar.activation(scores[:, i // 4, i % 4 * 512:(i % 4 + 1) * 512],
                                         ps[:, i, :], ACT.Copy).then_inc(sc_sb, 1)

                def take_hidden(b, s):
                    act.wait_ge(w_used, b + 1 + l * LAYER + MIX_BLOCKS)
                    nc.scalar.activation(arena[:, bass.ds(b * SEQ, SEQ)], ps[:, s, 0:SEQ],
                                         ACT.Gelu_apprx_tanh).then_inc(h_done, 1)

                def activate_hidden(b, s):
                    act.wait_ge(w_used, b + 1 + l * LAYER + MIX_BLOCKS)
                    nc.scalar.activation(ps[:, s, 0:SEQ], ps[:, s, 0:SEQ],
                                         ACT.Gelu_apprx_tanh).then_inc(h_psum, 1)

                def down(b, s):
                    high_part(b + l * LAYER + MIX_BLOCKS, s)
                    take_hidden(b - 2, (s - 2) % RAW)

                def late_down(b, s):
                    high_part(b + l * LAYER + MIX_BLOCKS, s)
                    activate_hidden(b - 2, (s - 2) % RAW)

                take_hidden(0, 0)
                take_hidden(1, 1)
                blocks(act, down, RAW, EXP_AT)
                act.wait_ge(best_done, l + 1)
                bb = ret[:, BEST_AT:BEST_AT + TILES * P]
                nc.scalar.activation(bb, bb, ACT.Exp).then_inc(gexp_done, 1)
                blocks(act, down, EXP_AT, G_FROM)
                for b in range(G_FROM, G_FROM + RAW):
                    (down if b < G_FROM + 2 else late_down)(b, b % RAW)
                blocks(act, late_down, G_FROM + RAW, BLOCKS)
                for b in range(2):
                    high_part(b + l * LAYER + UP_FROM, b)
                    activate_hidden(BLOCKS - 2 + b, RAW - 2 + b)

                def round_hidden(b, s):
                    nc.scalar.activation(hh[:, s, :], arena[:, bass.ds(b * SEQ, SEQ)],
                                         ACT.Copy).then_inc(ghhi_done, 1)

                def up(b, s):
                    high_part(b + l * LAYER + UP_FROM, s)
                    round_hidden(b, s)

                act.wait_ge(gmul_done, (l + 1) * TGROUPS)
                act.wait_ge(hmul_done, (l + 1) * (BLOCKS - G_FROM))
                for b in range(RAW):
                    if b >= 2:
                        high_part(b + l * LAYER + UP_FROM, b)
                    round_hidden(b, b)
                blocks(act, up, RAW, BLOCKS)
                if l + 1 < LAYERS:
                    high_parts((l + 1) * LAYER, (l + 1) * LAYER + RAW)
            act.wait_ge(x_ready, 8 * LAYERS)
            norm_stats(xs, hn)

        @block.tensor
        def _(pe):
            def mm(out, lhsT, rhs, start=True, stop=True, shared=False):
                return nc.tensor.matmul(out, lhsT, rhs, start=start, stop=stop, skip_group_check=shared)

            def transpose_tokens(src, bank, done):
                for i in range(DC // 2):
                    for c in (2 * i, 2 * i + 1):
                        for t in range(TILES):
                            o = (c % 2) * SEQ + t * P
                            last = nc.tensor.transpose(ps[:, bank + i, o:o + P],
                                                       src[:, t, c * P:(c + 1) * P], ident[:, :])
                    last.then_inc(done, 1)

            def weights(b, l):
                pe.wait_ge(whi_done, b + 1 + l * LAYER)
                pe.wait_ge(wlo_pool, b + 1 + l * UP_FROM)

            def tokens_times_block(b, c, s, banks, first, final):
                for t in range(TILES):
                    ts = slice(t * P, (t + 1) * P)
                    for k in range(2):
                        out = ps[:, banks + 2 * t + k, :]
                        ks = slice(k * 512, (k + 1) * 512)
                        mm(out, hh[:, c, ts], whs[:, s, ks], first, False)
                        mm(out, hh[:, c, ts], w_lo[:, s % WLO, ks], False, False)
                        last = mm(out, hl[:, c, ts], whs[:, s, ks], False, final)
                last.then_inc(w_used, 1)

            pe.wait_ge(consts_loaded, 32)
            for l in range(LAYERS):
                pe.wait_ge(hn_done, 4 * l + 2)
                transpose_tokens(hn, 0, hT_psum)
                for b in range(IN_BLOCKS):
                    f, c = divmod(b, DC)
                    pe.wait_ge(hl_done, 3 * DC * l + (DC if f else 2 * (c // 2) + 2))
                    weights(b, l)
                    tokens_times_block(b, c, b % RAW, 4 * (1 - f), c == 0, c == DC - 1)
                if l == 0:
                    pe.wait_ge(tabs_loaded, 112)
                    pe.wait_ge(proj_sb, 2 * NB)
                    for g in range(len(WINDOWS)):
                        o = 3 * 512 + g * P
                        for t in range(TILES):
                            last = mm(ps[:, 4 + g, 0:SEQ], proj[:, t, o:o + P], poolm[:, t, g, :],
                                      t == 0, t == TILES - 1)
                        last.then_inc(pool_psum, 1)
                    pe.wait_ge(rot_done, TILES)
                    transpose_tokens(proj, 0, qkT_psum)
                    for g in range(len(WINDOWS)):
                        pe.wait_ge(pooled_sb, g + 1)
                        mm(ps[:, 4 + g, SEQ:2 * SEQ], poolw[:, g, :], pooledT[:, g, :]
                           ).then_inc(poolmix_psum, 1)
                    pe.wait_ge(qkT_sb, DC // 2)
                    for h in range(HEADS):
                        if h == 4:
                            pe.wait_ge(hl_done, DC + len(WINDOWS))
                        r = slice(h % 2 * HD, (h % 2 + 1) * HD)
                        for t in range(TILES):
                            last = mm(ps[:, h, t * SEQ:(t + 1) * SEQ], qkT[r, h // 2, t * P:(t + 1) * P],
                                      qkT[r, 4 + h // 2, :])
                        last.then_inc(s_psum, 1)
                    for h in range(HEADS):
                        pe.wait_ge(p_done, TILES * (h + 1))
                        for k in range(TILES):
                            for t in range(TILES):
                                o = k * SEQ + t * P
                                last = nc.tensor.transpose(ps[:, h, o:o + P],
                                                           probs[:, h, t * SEQ + k * P:t * SEQ + (k + 1) * P],
                                                           ident[:, :])
                        last.then_inc(pT_psum, 1)
                    for j in range(HEADS // 2):
                        pe.wait_ge(pT_sb, 2 * j + 2)
                        for h in (2 * j, 2 * j + 1):
                            r = slice(h % 2 * HD, (h % 2 + 1) * HD)
                            for k in range(TILES):
                                v = proj[:, k, 2 * 512 + h * HD:2 * 512 + (h + 1) * HD]
                                last = mm(ps[r, j, 0:SEQ], v, probsT[:, h, k * SEQ:(k + 1) * SEQ],
                                          k == 0, k == TILES - 1)
                        last.then_inc(pv_psum, 1)
                else:
                    pe.wait_ge(sgu_loaded, 48)
                    for t in range(TILES):
                        pe.wait_ge(vn_done, t + 1)
                        for k in range(2):
                            for g in range(4 * k, 4 * k + 4):
                                o = g % 4 * P
                                last = mm(ps[:, 4 + 2 * t + k, o:o + P], ws[:, g, :],
                                          vn[:, t, g * P:(g + 1) * P])
                            last.then_inc(sgu_psum, 1)
                    pe.wait_ge(gated_done, 4)
                    transpose_tokens(u_sb, 0, gT_psum)
                for c in range(DC):
                    done = DC if l == 0 else 2 * (c // 2) + 2
                    pe.wait_ge(hl_done, DC * (3 * l + 1) + done)
                    weights(IN_BLOCKS + c, l)
                    tokens_times_block(IN_BLOCKS + c, c, c % RAW, 4, c == 0, c == DC - 1)

                pe.wait_ge(hn_done, 4 * l + 4)
                transpose_tokens(hn, 4, hT_psum)
                for b in range(Q_BLOCKS):
                    f, c = divmod(b, DC)
                    pe.wait_ge(hl_done, DC * (3 * l + 2) + (DC if f else 2 * (c // 2) + 2))
                    weights(Q_FROM + b, l)
                    s = b % RAW
                    for m in range(8):
                        out = ps[:, 4 * f + m // 2, m % 2 * SEQ:(m % 2 + 1) * SEQ]
                        ms = slice(m * P, (m + 1) * P)
                        mm(out, whs[:, s, ms], hh[:, c, :], c == 0 and m % 2 == 0, False, shared=True)
                        mm(out, whs[:, s, ms], hl[:, c, :], False, False, shared=True)
                        last = mm(out, w_lo[:, s % WLO, ms], hh[:, c, :], False, c == DC - 1, shared=True)
                    last.then_inc(w_used, 1)
                pe.wait_ge(subk_loaded, 16 * (l + 1))
                for t in range(TILES):
                    for n in range(HALVES):
                        if n % 4 == 0:
                            pe.wait_ge(qT_sb, 8 * l + (8 if t else max(4, n // 2 + 2)))
                        o = n % 4 * P
                        last = mm(ps[:, 4 * t + n // 4, o:o + P], qT[:, n, t * P:(t + 1) * P], subk[:, n, :])
                        if n % 4 == 3:
                            last.then_inc(sc_psum, 1)

                def down(b, s, when="early"):
                    weights(b + MIX_BLOCKS, l)
                    if when == "first":
                        pe.wait_ge(sc_sb, 8 * l + s + 1)
                    elif when == "early":
                        pe.wait_ge(h_done, b - RAW + 1 + l * G_FROM)
                    else:
                        pe.wait_ge(hmul_done, b - RAW + 1 - G_FROM + l * (BLOCKS - G_FROM))
                    for c in range(DC):
                        cs = slice(c * P, (c + 1) * P)
                        out = ps[:, s, 0:SEQ]
                        mm(out, whs[:, s, cs], hh[:, c, :], c == 0, False)
                        mm(out, whs[:, s, cs], hl[:, c, :], False, False)
                        last = mm(out, w_lo[:, s % WLO, cs], hh[:, c, :], False, c == DC - 1)
                    last.then_inc(w_used, 1)

                for b in range(RAW):
                    down(b, b, "first")
                blocks(pe, down, RAW, IDS_AT)
                pe.wait_ge(sc_sb, 8 * (l + 1))
                pe.wait_ge(idg_done, l + 1)
                for t in range(TILES):
                    nc.tensor.transpose(ps[:, 4, t * P:(t + 1) * P],
                                        ret[:, BEST_AT + t * P:BEST_AT + (t + 1) * P], ident[:, :])
                for t in range(TILES):
                    last = nc.tensor.transpose(ps[:, 4, SEQ + t * P:SEQ + (t + 1) * P], idf[:, t, :],
                                               ident[:, :])
                last.then_inc(idg_psum, 1)
                blocks(pe, down, IDS_AT, G_FROM)

                def token_gates(g, s, first=False):
                    pe.wait_ge(oh_built, (g + 1 + l * TGROUPS) * (TOK + 1))
                    if not first:
                        pe.wait_ge(gmul_done, g - 3 + l * TGROUPS)
                    for k in range(TOK):
                        last = mm(ps[:, 4 + s, k * P:(k + 1) * P], oh2[:, s % 2, k, :], oh1g[:, s % 2, k, :])
                    last.then_inc(g_mm, 1)

                for j in range(RAW):
                    down(G_FROM + j, j)
                    token_gates(j, j, first=True)
                with pe.Fori(1, TGROUPS // RAW) as i:
                    for j in range(RAW):
                        down(G_FROM + i * RAW + j, j, "late")
                        token_gates(i * RAW + j, j)
                blocks(pe, lambda b, s: down(b, s, "late"), G_TO, BLOCKS)

                def up(b, s, first=False, final=False):
                    pe.wait_ge(wlo_dve, b + l * BLOCKS + 1)
                    pe.wait_ge(ghlo_done, b + l * BLOCKS + 1)
                    tokens_times_block(b, s, s, 0, first, final)

                for b in range(RAW):
                    up(b, b, first=b == 0)
                blocks(pe, up, RAW, BLOCKS - RAW)
                for b in range(BLOCKS - RAW, BLOCKS):
                    up(b, b % RAW, final=b == BLOCKS - 1)

        @block.vector
        def _(dve):
            steps = [0]
            norms = [0]

            def step(ins):
                steps[0] += 1
                return ins.then_inc(dve_step, 1)

            def settle():
                dve.wait_ge(dve_step, steps[0])

            def norm_scale():
                norms[0] += 1
                dve.wait_ge(sumsq_done, TILES * norms[0])
                nc.vector.tensor_scalar(meansq[:, :], sumsq[:, :], 1.0 / DM, EPS, ALU.mult,
                                        ALU.add).then_inc(ms_done, 1)
                dve.wait_ge(std_done, norms[0])
                dve.wait_ge(ms_done, norms[0])
                step(nc.vector.reciprocal(rinv[:, :], std[:, :]))
                settle()
                step(nc.vector.tensor_tensor(rtmp[:, :], rinv[:, :], rinv[:, :], ALU.mult))
                settle()
                step(nc.vector.tensor_tensor(rtmp[:, :], rtmp[:, :], meansq[:, :], ALU.mult))
                settle()
                step(nc.vector.tensor_scalar(rtmp[:, :], rtmp[:, :], -0.5, 1.5, ALU.mult, ALU.add))
                settle()
                step(nc.vector.tensor_tensor(rinv[:, :], rinv[:, :], rtmp[:, :], ALU.mult))
                settle()

            def norm_tokens():
                norm_scale()
                for t in range(TILES):
                    nc.vector.tensor_scalar(hn[:, t, :], xs[:, t, :], rinv[:, t:t + 1], None,
                                            ALU.mult).then_inc(hn_done, 1)

            hh_seen = [0]

            def split_chunks(chunks, bank_of, scale):
                for i, c in enumerate(chunks):
                    hh_need = hh_seen[0] + (i // 2 * 2 + 2)
                    dve.wait_ge(hh_done, hh_need)
                    bank, o = bank_of(c)
                    src = ps[:, bank, o:o + SEQ]
                    if scale is None:
                        ins = nc.vector.tensor_tensor(hl[:, c, :], src, hh[:, c, :].bitcast(F32), ALU.subtract)
                    else:
                        ins = nc.vector.scalar_tensor_tensor(hl[:, c, :], src, scale(c),
                                                             hh[:, c, :].bitcast(F32), ALU.mult, ALU.subtract)
                    ins.then_inc(hl_done, 1)
                hh_seen[0] += len(chunks)

            def paired(bank):
                return lambda c: (bank + c // 2, c % 2 * SEQ)

            def add_residual(done, count, bank):
                dve.wait_ge(done, count)
                for i in range(4):
                    t, k = divmod(i, 2)
                    part = xs[:, t, k * 512:(k + 1) * 512]
                    nc.vector.tensor_tensor(part, part, ps[:, bank + i, :], ALU.add).then_inc(x_ready, 1)

            dve.wait_ge(x_loaded, 16)
            for l in range(LAYERS):
                if l:
                    dve.wait_ge(x_ready, 8 * l)
                norm_tokens()
                if l == 0:
                    dve.wait_ge(consts_loaded, 32)
                split_chunks(range(DC), paired(0), lambda c: gam[:, 2 * l, c:c + 1])
                if l == 0:
                    dve.wait_ge(tabs_loaded, 112)
                    for t in range(TILES):
                        dve.wait_ge(proj_sb, 2 * (t + 1))
                        qk = proj[:, t, 0:2 * 512].rearrange("p (h d) -> p h d", d=HD)
                        t1, t2 = qk[:, :, 0:ROT], qk[:, :, ROT:2 * ROT]
                        cos = tab[:, 0, t, :].unsqueeze(1).to_broadcast([P, 2 * HEADS, ROT])
                        sin = tab[:, 1, t, :].unsqueeze(1).to_broadcast([P, 2 * HEADS, ROT])
                        if t:
                            dve.wait_ge(rot_done, t)
                        step(nc.vector.tensor_tensor(rot[:, 0], t1, cos, ALU.mult))
                        step(nc.vector.tensor_tensor(rot[:, 1], t2, sin, ALU.mult))
                        step(nc.vector.tensor_tensor(rot[:, 2], t2, cos, ALU.mult))
                        step(nc.vector.tensor_tensor(rot[:, 3], t1, sin, ALU.mult))
                        settle()
                        step(nc.vector.tensor_tensor(t1, rot[:, 0], rot[:, 1], ALU.subtract))
                        settle()
                        nc.vector.tensor_tensor(t2, rot[:, 2], rot[:, 3], ALU.add).then_inc(rot_done, 1)
                    for i in range(DC // 2):
                        dve.wait_ge(qkT_psum, i + 1)
                        nc.vector.tensor_copy(qkT[:, 2 * i:2 * i + 2, :],
                                              ps[:, i, :].rearrange("p (c t) -> p c t", t=SEQ)
                                              ).then_inc(qkT_sb, 1)
                    for g in range(len(WINDOWS)):
                        dve.wait_ge(hh_done, hh_seen[0] + g + 1)
                        nc.vector.scalar_tensor_tensor(
                            hl[:, 4 + g, :], ps[:, 4 + g, SEQ:2 * SEQ], pscale[:, g:g + 1],
                            hh[:, 4 + g, :].bitcast(F32), ALU.mult, ALU.subtract).then_inc(hl_done, 1)
                    hh_seen[0] += len(WINDOWS)

                    def weigh(h):
                        dve.wait_ge(s_psum, h + 1)
                        step(nc.vector.scalar_tensor_tensor(probs[:, h, :], ps[:, h, :], HD ** -0.5,
                                                            lncount, ALU.mult, ALU.add))
                        settle()
                        step(nc.vector.reduce_max(rowmax[:, h, :], probs[:, h, :].rearrange(
                            "p (t k) -> p t k", k=SEQ), AX.X))
                        settle()
                        nc.vector.tensor_scalar(rowmax[:, h, :], rowmax[:, h, :], -1.0, None,
                                                ALU.mult).then_inc(nmax_done, 1)

                    def normalise(h):
                        dve.wait_ge(exp_done, TILES * (h + 1))
                        step(nc.vector.reciprocal(rowinv[:, h, :], rowsum[:, h, :]))
                        settle()
                        for t in range(TILES):
                            p = probs[:, h, t * SEQ:(t + 1) * SEQ]
                            nc.vector.tensor_scalar(p, p, rowinv[:, h, t:t + 1], None,
                                                    ALU.mult).then_inc(p_done, 1)

                    for h in range(HEADS):
                        weigh(h)
                        if h:
                            normalise(h - 1)
                    normalise(HEADS - 1)
                    for j in range(HEADS // 2):
                        dve.wait_ge(hh_done, hh_seen[0] + j + 1)
                        nc.vector.tensor_tensor(hl[:, j, :], ps[:, j, 0:SEQ], hh[:, j, :].bitcast(F32),
                                                ALU.subtract).then_inc(hl_done, 1)
                    hh_seen[0] += HEADS // 2
                else:
                    norm_scale()
                    dve.wait_ge(sgu_loaded, 48)
                    for t in range(TILES):
                        nc.vector.scalar_tensor_tensor(vn[:, t, :], v_sb[:, t, :], rinv[:, t:t + 1], cnorm,
                                                       ALU.mult, ALU.mult).then_inc(vn_done, 1)
                    for i in range(4):
                        t, k = divmod(i, 2)
                        dve.wait_ge(sgu_psum, i + 1)
                        for g in range(4 * k, 4 * k + 4):
                            part = u_sb[:, t, g * P:(g + 1) * P]
                            o = g % 4 * P
                            last = nc.vector.scalar_tensor_tensor(part, ps[:, 4 + i, o:o + P], bs[:, g:g + 1],
                                                                  part, ALU.add, ALU.mult)
                            if g % 4 < 3:
                                step(last)
                        last.then_inc(gated_done, 1)
                    split_chunks(range(DC), paired(0), None)
                add_residual(w_used, l * LAYER + Q_FROM, 4)

                dve.wait_ge(x_ready, 8 * l + 4)
                norm_tokens()
                split_chunks(range(DC), paired(4), lambda c: gam[:, 2 * l + 1, c:c + 1])

                def top16(rows):
                    for r in range(0, len(rows), 4):
                        some = rows[r:r + 4]
                        for half in (slice(0, 8), slice(8, 16)):
                            settle()
                            for vals, top, pos in some:
                                step(nc.vector.max(top[:, half], vals))
                            settle()
                            for vals, top, pos in some:
                                step(nc.vector.max_index(pos[:, half], top[:, half], vals))
                            if half.start == 0:
                                settle()
                                for vals, top, pos in some:
                                    step(nc.vector.match_replace(vals, top[:, half], vals, LOWEST))

                for t in range(TILES):
                    dve.wait_ge(sc_sb, 8 * l + 4 * (t + 1))
                    top16([(scores[:, t, n * KEYS:(n + 1) * KEYS], sv[:, t, n, :], si[:, t, n, :])
                           for n in range(HALVES)])
                    settle()
                    step(nc.vector.tensor_copy(sif[:, t].rearrange("p h i k -> p (h i) k"), si[:, t]))
                    settle()
                    step(nc.vector.tensor_scalar(sif[:, t, :, 0, :], sif[:, t, :, 0, :], float(KEYS), None,
                                                 ALU.mult))
                    settle()
                    svt = sv[:, t].rearrange("p (h i) k -> p h i k", i=2)
                    o = 0
                    for a0, a1, nb in SEGS:
                        na = a1 - a0
                        for dst, src in ((cand, svt), (pay, sif[:, t])):
                            d = dst[:, :, o:o + na * nb].rearrange("p h (a b) -> p h a b", b=nb)
                            f = src[:, :, 0, a0:a1].unsqueeze(3).to_broadcast([P, RH, na, nb])
                            s = src[:, :, 1, 0:nb].unsqueeze(2).to_broadcast([P, RH, na, nb])
                            step(nc.vector.tensor_tensor(d, f, s, ALU.add))
                        o += na * nb
                    top16([(cand[:, h, :], best[:, t, h, :], ci[:, t, h, :]) for h in range(RH)])
                    settle()
                    step(nc.vector.tensor_copy(cif[:, t], ci[:, t].rearrange("p h k -> p (h k)")))
                    settle()
                    for h in range(0, RH, 2):
                        n = 2 * TOPK
                        step(nc.vector.tensor_tensor(
                            eq, iotac[:, :].unsqueeze(1).to_broadcast([P, n, CAND]),
                            cif[:, t, h * TOPK:h * TOPK + n].unsqueeze(2).to_broadcast([P, n, CAND]),
                            ALU.is_equal))
                        settle()
                        e4 = eq.rearrange("p (h k) c -> p h k c", k=TOPK)
                        step(nc.vector.tensor_tensor(
                            e4, e4, pay[:, h:h + 2, :].unsqueeze(2).to_broadcast([P, 2, TOPK, CAND]),
                            ALU.mult))
                        settle()
                        step(nc.vector.reduce_sum(idf[:, t, h * TOPK:h * TOPK + n], eq, AX.X))
                        settle()
                b3 = best.rearrange("p t h k -> p (t h) k")
                gs = gsum[:, :, :].rearrange("p a h -> p (a h)")
                top, tot = gs[:, 0:TILES * RH], gs[:, TILES * RH:2 * TILES * RH]
                wide = [P, TILES * RH, TOPK]
                step(nc.vector.tensor_copy(top, b3[:, :, 0]))
                settle()
                nc.vector.tensor_tensor(b3, b3, top.unsqueeze(2).to_broadcast(wide),
                                        ALU.subtract).then_inc(best_done, 1)
                dve.wait_ge(gexp_done, l + 1)
                step(nc.vector.reduce_sum(tot, b3, AX.X))
                settle()
                step(nc.vector.reciprocal(tot, tot))
                settle()
                nc.vector.tensor_tensor(b3, b3, tot.unsqueeze(2).to_broadcast(wide),
                                        ALU.mult).then_inc(idg_done, 1)
                settle()
                step(nc.vector.memset(arena[:, G_FROM * SEQ:BLOCKS * SEQ], 1.0))
                dve.wait_ge(idg_psum, l + 1)
                step(nc.vector.tensor_copy(gT, ps[:, 4, 0:SEQ]))
                step(nc.vector.tensor_copy(idi, ps[:, 4, SEQ:2 * SEQ]))
                settle()
                step(nc.vector.tensor_scalar(idk, idi, 7, None, ALU.arith_shift_right))
                settle()
                step(nc.vector.tensor_copy(i1T, idk))
                step(nc.vector.tensor_scalar(idi, idi, KEYS - 1, None, ALU.bitwise_and))
                settle()
                step(nc.vector.tensor_copy(i2T, idi))
                settle()

                def low_part(b, s):
                    n = b + l * LAYER + UP_FROM
                    dve.wait_ge(whi_done, n + 1)
                    dve.wait_ge(w_used, n - WLO + 1)
                    nc.vector.tensor_tensor(w_lo[:, s % WLO, :], raw[:, s, :], whs[:, s].bitcast(F32),
                                            ALU.subtract).then_inc(wlo_dve, 1)

                gates_before, hiddens_before = l * TGROUPS, l * (BLOCKS - G_FROM)

                def build_first(g, s, first=False):
                    if not first:
                        dve.wait_ge(g_mm, g - 1 + gates_before)
                    for k in range(TOK):
                        t = bass.ds(g * TOK + k, 1)
                        nc.vector.tensor_scalar(oh1g[:, s, k, :], iota[:, :], i1T[:, t], gT[:, t],
                                                ALU.is_equal, ALU.mult).then_inc(oh_built, 1)

                def build_second(g, s):
                    keys = i2T[:, bass.ds(g * TOK, TOK)].unsqueeze(2).to_broadcast([P, TOK, P])
                    nc.vector.tensor_tensor(oh2[:, s], iota3, keys, ALU.is_equal).then_inc(oh_built, 1)

                def gate(g, s, hiddens):
                    dve.wait_ge(g_mm, g + 1 + gates_before)
                    if hiddens is not None:
                        dve.wait_ge(hmul_done, hiddens + hiddens_before)
                    part = H[:, :, bass.ds(g * TOK, TOK)]
                    nc.vector.tensor_tensor(part, part, ps[:, 4 + s, :].rearrange("p (t i) -> p i t", t=TOK),
                                            ALU.mult).then_inc(gmul_done, 1)

                def hidden(b, s, gates=TGROUPS):
                    dve.wait_ge(h_psum, b - G_FROM + 1 + hiddens_before)
                    dve.wait_ge(gmul_done, gates + gates_before)
                    part = arena[:, bass.ds(b * SEQ, SEQ)]
                    nc.vector.tensor_tensor(part, part, ps[:, s, 0:SEQ], ALU.mult).then_inc(hmul_done, 1)

                def turn(g, j):
                    build_first(g + 1, (j + 1) % 2)
                    hidden(g + (G_FROM - 2), (j - 2) % RAW, gates=g)
                    build_second(g + 1, (j + 1) % 2)
                    gate(g, j, hiddens=g - 1)

                build_first(0, 0, first=True)
                build_second(0, 0)
                build_first(1, 1, first=True)
                build_second(1, 1)
                dve.wait_ge(h_done, (l + 1) * G_FROM)
                gate(0, 0, None)
                build_first(2, 0)
                build_second(2, 0)
                gate(1, 1, None)
                turn(2, 2)
                turn(3, 3)
                with dve.Fori(1, TGROUPS // RAW - 1) as i:
                    for j in range(RAW):
                        turn(i * RAW + j, j)
                for g in range(TGROUPS - RAW, TGROUPS - 1):
                    turn(g, g % RAW)
                hidden(G_TO - 3, (G_TO - 3) % RAW, gates=TGROUPS - 1)
                gate(TGROUPS - 1, (TGROUPS - 1) % RAW, hiddens=TGROUPS - 2)
                blocks(dve, lambda b, s: hidden(b - 2, (s - 2) % RAW), G_TO, BLOCKS)
                for b in range(2):
                    low_part(b, b)
                    hidden(BLOCKS - 2 + b, RAW - 2 + b)

                def low_hidden(b, s):
                    dve.wait_ge(ghhi_done, b + l * BLOCKS + 1)
                    nc.vector.tensor_tensor(hl[:, s, :], arena[:, bass.ds(b * SEQ, SEQ)],
                                            hh[:, s, :].bitcast(F32), ALU.subtract).then_inc(ghlo_done, 1)

                def up(b, s):
                    low_part(b, s)
                    low_hidden(b, s)

                for b in range(RAW):
                    if b >= 2:
                        low_part(b, b)
                    low_hidden(b, b)
                blocks(dve, up, RAW, BLOCKS)
                add_residual(w_used, (l + 1) * LAYER, 0)
            dve.wait_ge(x_ready, 8 * LAYERS)
            norm_scale()
            dve.wait_ge(gfin_loaded, 16)
            for t in range(TILES):
                nc.vector.scalar_tensor_tensor(hn[:, t, :], xs[:, t, :], rinv[:, t:t + 1], cnorm, ALU.mult,
                                               ALU.mult).then_inc(hn_done, 1)


def shape_tables():
    f = np.float32
    pos = np.arange(SEQ, dtype=f)
    inv = (f(500000.0) ** (-np.arange(0, 2 * ROT, 2, dtype=f) / f(2 * ROT))).astype(f)
    ang = (pos[:, None] * inv[None, :]).astype(f)
    tab = np.stack([np.cos(ang), np.sin(ang)]).astype(f).reshape(2, TILES, P, ROT).transpose(2, 0, 1, 3)
    rel = np.abs(np.arange(SEQ)[:, None] - np.arange(SEQ)[None, :])
    count = sum(((rel % dil == 0) & (rel <= window // 2)).astype(np.float64) for window, dil in PATTERNS)
    lncount = np.where(count > 0, np.log(np.maximum(count, 1)), -1e30).astype(f)
    lncount = lncount.reshape(TILES, P, SEQ).transpose(1, 0, 2).reshape(P, TILES * SEQ)
    poolm = np.zeros((SEQ, len(WINDOWS), SEQ), f)
    for g, win in enumerate(WINDOWS):
        for t in range(SEQ):
            lo, hi = max(t - win // 2, 0), min(t + win - win // 2, SEQ)
            poolm[lo:hi, g, t] = 1.0 / (hi - lo)
            poolm[t, g, t] -= 1.0
    poolm = poolm.reshape(TILES, P, len(WINDOWS), SEQ).transpose(1, 0, 2, 3)
    ones = np.ones((P, 1), f)
    return {"tab": tab, "lncount": lncount, "poolm": poolm, "ident": np.eye(P, dtype=f),
            "iota": ones * np.arange(P, dtype=f), "iotac": ones * np.arange(CAND, dtype=f)}


def kernel(**inputs):
    import numpy as _np
    import concourse.bacc as _bacc
    from concourse import mybir as _mybir
    from concourse.bass_utils import run_bass_kernel_spmd as _run

    a = {k: _np.asarray(v) for k, v in inputs.items()}

    def column_blocks(w):
        w = w.reshape(LAYERS, DC, P, -1, DM).transpose(0, 3, 1, 2, 4)
        return w.reshape(LAYERS, -1, P, DM)

    gammas = _np.stack([a["norm_mix"], a["norm_ffn"]], axis=1).reshape(2 * LAYERS, DC, P)
    arrays = {
        "x": a["x"].reshape(TILES, P, DM).transpose(1, 0, 2),
        "gam": gammas.transpose(2, 0, 1),
        "gfin": _np.broadcast_to(a["norm_final"], (P, DM)),
        **shape_tables(),
        "poolw": a["pool_w"][0].transpose(1, 0, 2),
        "pscale": a["pool_scale"].reshape(len(WINDOWS), P).transpose(1, 0),
        "wm": _np.concatenate([column_blocks(_np.concatenate([a["ab_w_in"], a["c_w_in"]])),
                               column_blocks(_np.concatenate([a["ab_w_out"], a["c_w_out"]])),
                               column_blocks(a["peer_w_q"])], axis=1),
        "ws": a["c_w_s"][0].transpose(2, 0, 1),
        "bs": a["c_b_s"][0].transpose(1, 0),
        "cnorm": _np.broadcast_to(a["c_norm"].reshape(DM), (P, DM)),
        "subk": a["peer_sub_keys"].reshape(LAYERS, HALVES, KEYS, P).transpose(0, 3, 1, 2),
        "wd": a["peer_w_down"].reshape(LAYERS, BLOCKS, KEYS, DC, P).transpose(0, 1, 4, 3, 2).reshape(
            LAYERS, BLOCKS, P, DM),
        "wu": a["peer_w_up"].reshape(LAYERS, BLOCKS, KEYS, DM),
    }
    order = ["x", "gam", "gfin", "tab", "ident", "iota", "iotac", "lncount", "poolm", "poolw", "pscale",
             "wm", "ws", "bs", "cnorm", "subk", "wd", "wu"]
    nc = _bacc.Bacc("TRN2", target_bir_lowering=False, num_devices=1)
    feeds, args = {}, []
    for name in order:
        arr = _np.ascontiguousarray(arrays[name])
        feeds[f"in_{name}"] = arr
        args.append(nc.dram_tensor(f"in_{name}", arr.shape, _mybir.dt.from_np(arr.dtype),
                                   kind="ExternalInput").ap())
    out = nc.dram_tensor("out", (P, TILES, DM), _mybir.dt.float32, kind="ExternalOutput").ap()
    build_trunk(nc, *args, out)
    r = _run(nc, [feeds], core_ids=[0])
    return r.results[0]["out"].transpose(1, 0, 2).reshape(1, SEQ, DM)
```

```python
from contextlib import ExitStack

import numpy as np

import concourse.bass as bass
from concourse import mybir

F32 = mybir.dt.float32
F32R = mybir.dt.float32r
I32 = mybir.dt.int32
U32 = mybir.dt.uint32
ALU = mybir.AluOpType
ACT = mybir.ActivationFunctionType
AX = mybir.AxisListType

P = 128
LAYERS = 2
SEQ = 256
TILES = SEQ // P
DM = 1024
DC = DM // P
PROJ = 2048
NB = PROJ // 512
EPS = 1e-6
HALF = DM // 2
QUARTERS = 4

HEADS = 8
HD = 64
ROT = HD // 8
WINDOWS = (2, 4, 8, 16)
PATTERNS = ((128, 1), (512, 4), (2048, 16))
GROUPS = 8

RH = 8
HALVES = 2 * RH
KEYS = 128
TOPK = 16
SEGS = ((0, 1, 16), (1, 2, 8), (2, 4, 5), (4, 8, 3), (8, 16, 1))
CAND = sum((a1 - a0) * nb for a0, a1, nb in SEGS)
LOWEST = -3.0e38

BLOCKS = KEYS
RAW = 4
WHI = 4
WLO = 2
GHS = 4
TOK = 4
TGROUPS = SEQ // TOK
IN_BLOCKS, OUT_BLOCKS, Q_BLOCKS = 16, 8, 16
MIX_BLOCKS = IN_BLOCKS + OUT_BLOCKS + Q_BLOCKS
Q_FROM = IN_BLOCKS + OUT_BLOCKS
UP_FROM = MIX_BLOCKS + BLOCKS
LAYER = UP_FROM + BLOCKS
EXP_AT = 40
IDS_AT = 44
G_FROM = 56
G_TO = G_FROM + TGROUPS
TURN_QK, SCORE_BEFORE = 11, (12, 15)
MIX_BEFORE = 14

SUBK_AT = 0
WS_AT = 2048
CN_AT = 3072
BS_AT = 4096
POOLM_AT = 4608
POOLED_AT = 6656
POOLW_AT = 7680
LN_AT = 8192
ROT_AT = 8704
QT_AT = 9216
PROJ_AT = 16384
QKT_AT = 20480
VN_AT = 20480
PR_AT = 22528
PT_AT = 26624
HN_AT = 30720
EQ_AT = 24448
SV_AT = 26176
SI_AT = 26688
SIF_AT = 27200
CD_AT = 27712
PAY_AT = 28144
SC_AT = 28672
SMALL_FREE_AT = 20
assert EQ_AT + 32 * CAND <= SV_AT and PAY_AT + RH * CAND <= SC_AT and G_FROM * SEQ <= EQ_AT
assert BS_AT + GROUPS <= SMALL_FREE_AT * SEQ
BEST_AT, CIF_AT, IDF_AT, CI_AT = 1024, 1280, 1536, 1792


def build_trunk(nc, x_d, gam_d, gfin_d, tab_d, ident_d, iota_d, iotac_d, lncount_d, poolm_d, poolw_d,
                pscale_d, wm_d, ws_d, bs_d, cnorm_d, subk_d, wd_d, wu_d, out_d):
    ctx = ExitStack()
    with ctx:
        def sb(name, shape, dt):
            return ctx.enter_context(nc.sbuf_tensor(name, shape, dt))

        def sem(name):
            return ctx.enter_context(nc.semaphore(name))

        arena = sb("arena", [P, BLOCKS * SEQ], F32)
        xs = sb("xs", [P, TILES, DM], F32)
        ret = sb("ret", [P, DC * SEQ], F32)
        oh_buf = sb("oh_buf", [P, 2 * TOK * P], F32)
        hT_hi = sb("hT_hi", [P, DC * SEQ], F32R)
        hT_lo = sb("hT_lo", [P, DC * SEQ], F32R)
        raw = sb("raw", [P, RAW, DM], F32)
        w_hi = sb("w_hi", [P, WHI * DM], F32R)
        w_lo = sb("w_lo", [P, WLO, DM], F32R)
        ident = sb("ident", [P, P], F32)
        iota = sb("iota", [P, P], F32)
        iotac = sb("iotac", [P, CAND], F32)
        gam = sb("gam", [P, 2 * LAYERS, DC], F32)
        tab = sb("tab", [P, 2, TILES, ROT], F32)
        pscale = sb("pscale", [P, len(WINDOWS)], F32)
        sumsq = sb("sumsq", [P, 2, TILES], F32)
        total = sb("total", [P, TILES], F32)
        std = sb("std", [P, TILES], F32)
        primed = sb("primed", [P, 1], F32)
        rinv = sb("rinv", [P, 3, TILES], F32)
        rtmp = sb("rtmp", [P, TILES], F32)
        rowmax = sb("rowmax", [P, HEADS, TILES], F32)
        rowsum = sb("rowsum", [P, HEADS, TILES], F32)
        rowinv = sb("rowinv", [P, HEADS, TILES], F32)
        gsum = sb("gsum", [P, 2 * TILES, RH], F32)
        ps = ctx.enter_context(nc.psum_tensor("ps", [P, 8, 512], F32))

        def at(start, *dims):
            size = int(np.prod(dims))
            v = arena[:, start:start + size]
            if len(dims) == 1:
                return v
            names = "abcd"[:len(dims)]
            return v.rearrange(f"p ({' '.join(names)}) -> p {' '.join(names)}",
                               **{k: d for k, d in zip(names, dims)})

        H = arena[:, :].rearrange("p (i t) -> p i t", t=SEQ)
        rot = at(ROT_AT, 4, 2 * HEADS, ROT)
        proj = at(PROJ_AT, TILES, PROJ)
        u_sb = at(PROJ_AT, TILES, DM)
        v_sb = at(PROJ_AT + TILES * DM, TILES, DM)
        vn = at(VN_AT, TILES, DM)
        qkT = at(QKT_AT, DC, SEQ)
        probs = at(PR_AT, HEADS, TILES * SEQ)
        probsT = at(PT_AT, HEADS, TILES * SEQ)
        poolm = at(POOLM_AT, TILES, len(WINDOWS), SEQ)
        pooledT = at(POOLED_AT, len(WINDOWS), SEQ)
        ws = at(WS_AT, GROUPS, P)
        cnorm = at(CN_AT, DM)
        bs = at(BS_AT, GROUPS)
        hn = at(HN_AT, TILES, DM)
        qT = at(QT_AT, HALVES, SEQ)
        subk = at(SUBK_AT, HALVES, KEYS)
        scores = at(SC_AT, TILES, HALVES * KEYS)
        sv = at(SV_AT, TILES, HALVES, TOPK)
        si = arena[:, SI_AT:SI_AT + TILES * HALVES * TOPK].bitcast(U32).rearrange(
            "p (a b c) -> p a b c", a=TILES, b=HALVES)
        sif = at(SIF_AT, TILES, RH, 2, TOPK)
        cand = at(CD_AT, RH, CAND)
        pay = at(PAY_AT, RH, CAND)
        eq = at(EQ_AT, 2 * TOPK, CAND)
        lncount = at(LN_AT, TILES * SEQ)
        poolw = at(POOLW_AT, len(WINDOWS), P)

        i1T, i2T, gT = ret[:, 0:SEQ], ret[:, SEQ:2 * SEQ], ret[:, 2 * SEQ:3 * SEQ]
        best = ret[:, BEST_AT:BEST_AT + TILES * P].rearrange("p (t h k) -> p t h k", t=TILES, h=RH)
        cif = ret[:, CIF_AT:CIF_AT + TILES * P].rearrange("p (t n) -> p t n", t=TILES)
        idf = ret[:, IDF_AT:IDF_AT + TILES * P].rearrange("p (t n) -> p t n", t=TILES)
        ci = ret[:, CI_AT:CI_AT + TILES * P].bitcast(U32).rearrange("p (t h k) -> p t h k", t=TILES, h=RH)
        idi = ret[:, CIF_AT:CIF_AT + SEQ].bitcast(I32)
        idk = ret[:, CI_AT:CI_AT + SEQ].bitcast(I32)

        hh = hT_hi[:, :].rearrange("p (c t) -> p c t", t=SEQ)
        hl = hT_lo[:, :].rearrange("p (c t) -> p c t", t=SEQ)
        whs = w_hi[:, :].rearrange("p (s n) -> p s n", s=WHI)
        def ring(v):
            return v.rearrange("p (s t i) -> p s t i", s=2, t=TOK)

        oh2 = ring(ret[:, BEST_AT:BEST_AT + 2 * TOK * P])
        oh1g = ring(oh_buf[:, :])

        x_loaded = [sem(f"x_loaded{k}") for k in range(2)]
        consts_loaded, tabs_loaded = sem("consts_loaded"), sem("tabs_loaded")
        subk_loaded = sem("subk_loaded")
        sgu_loaded, gfin_loaded = sem("sgu_loaded"), sem("gfin_loaded")
        raw_full = [sem(f"raw_full{s}") for s in range(RAW)]
        out_stored = sem("out_stored")
        sumsq_done, total_done, std_done, rinv_done = (
            sem("sumsq_done"), sem("total_done"), sem("std_done"), sem("rinv_done"))
        hn_done, hT_psum = sem("hn_done"), sem("hT_psum")
        hh_done, hl_done = sem("hh_done"), sem("hl_done")
        tile_summed, x_ready = sem("tile_summed"), sem("x_ready")
        prime_done = sem("prime_done")
        scaled_pool, scaled_act = sem("scaled_pool"), sem("scaled_act")
        proj_sb = sem("proj_sb")
        pool_psum, pooled_sb, poolmix_psum = sem("pool_psum"), sem("pooled_sb"), sem("poolmix_psum")
        rot_done, qkT_psum, qkT_sb = sem("rot_done"), sem("qkT_psum"), sem("qkT_sb")
        s_psum, nmax_done, exp_done, p_done = sem("s_psum"), sem("nmax_done"), sem("exp_done"), sem("p_done")
        pT_psum, pT_sb, pv_psum = sem("pT_psum"), sem("pT_sb"), sem("pv_psum")
        vn_done, sgu_psum, gated_done = sem("vn_done"), sem("sgu_psum"), sem("gated_done")
        gT_psum = sem("gT_psum")
        q_summed, qT_sb, sc_psum, sc_sb = sem("q_summed"), sem("qT_sb"), sem("sc_psum"), sem("sc_sb")
        best_done, gexp_done, idg_done, idg_psum = (
            sem("best_done"), sem("gexp_done"), sem("idg_done"), sem("idg_psum"))
        whi_done, wlo_pool, wlo_dve, w_used = sem("whi_done"), sem("wlo_pool"), sem("wlo_dve"), sem("w_used")
        h_done, h_psum, hmul_done = sem("h_done"), sem("h_psum"), sem("hmul_done")
        chunks_free = sem("chunks_free")
        ghhi_done, ghlo_done = sem("ghhi_done"), sem("ghlo_done")
        oh_built, g_mm, gmul_done = sem("oh_built"), sem("g_mm"), sem("gmul_done")
        dve_step = sem("dve_step")
        iota3 = iota[:, :].unsqueeze(1).to_broadcast([P, TOK, P])

        def blocks(eng, body, first, last):
            with eng.Fori(first // RAW, last // RAW) as i:
                for j in range(RAW):
                    body(i * RAW + j, j)

        block = ctx.enter_context(nc.Block())


        @block.sync
        def _(sp):
            for l in range(LAYERS):
                def load(src, row, used, count, s):
                    sp.wait_ge(used, count)
                    sp.dma_start(raw[:, s, :], src[l, bass.ds(row, 1)].rearrange("b p n -> p (b n)")
                                 ).then_inc(raw_full[s], 16)

                for s in range(RAW):
                    if l:
                        sp.wait_ge(wlo_dve, l * BLOCKS - RAW + 1 + s)
                    if l == 0 and s in (0, 2):
                        k = s // 2
                        ks = slice(k * HALF, (k + 1) * HALF)
                        sp.dma_start(xs[:, :, ks], x_d[:, :, ks]).then_inc(x_loaded[k], 16)
                        if k == 0:
                            sp.dma_start(ident[:, :], ident_d).then_inc(consts_loaded, 16)
                            sp.dma_start(gam[:, :, :], gam_d).then_inc(consts_loaded, 16)
                    sp.dma_start(raw[:, s, :], wm_d[l, s]).then_inc(raw_full[s], 16)
                if l == 0:
                    sp.dma_start(tab[:, :, :, :], tab_d).then_inc(tabs_loaded, 16)
                    sp.dma_start(pscale[:, :], pscale_d).then_inc(tabs_loaded, 16)
                    sp.dma_start(iota[:, :], iota_d).then_inc(tabs_loaded, 16)
                    sp.dma_start(iotac[:, :], iotac_d).then_inc(tabs_loaded, 16)
                    sp.dma_start(poolm, poolm_d).then_inc(tabs_loaded, 16)
                    sp.dma_start(poolw, poolw_d).then_inc(tabs_loaded, 16)
                    sp.dma_start(lncount, lncount_d).then_inc(tabs_loaded, 16)
                    sp.dma_start(subk, subk_d[l]).then_inc(subk_loaded, 16)
                blocks(sp, lambda b, s: load(wm_d, b, wlo_pool, l * UP_FROM + b - RAW + 1, s),
                       RAW, MIX_BLOCKS)
                blocks(sp, lambda b, s: load(wd_d, b, wlo_pool, l * UP_FROM + MIX_BLOCKS + b - RAW + 1, s),
                       0, BLOCKS)
                for s in range(RAW):
                    sp.wait_ge(wlo_pool, (l + 1) * UP_FROM - RAW + 1 + s)
                    sp.dma_start(raw[:, s, :], wu_d[l, s]).then_inc(raw_full[s], 16)

                def load_up(b, s):
                    load(wu_d, b, wlo_dve, l * BLOCKS + b - RAW + 1, s)

                blocks(sp, load_up, RAW, 2 * SMALL_FREE_AT)
                sp.wait_ge(ghlo_done, l * BLOCKS + SMALL_FREE_AT)
                if l == 0:
                    sp.dma_start(ws, ws_d).then_inc(sgu_loaded, 16)
                    sp.dma_start(bs, bs_d).then_inc(sgu_loaded, 16)
                    sp.dma_start(cnorm, cnorm_d).then_inc(sgu_loaded, 16)
                    sp.dma_start(subk, subk_d[1]).then_inc(subk_loaded, 16)
                else:
                    sp.dma_start(cnorm, gfin_d).then_inc(gfin_loaded, 16)
                blocks(sp, load_up, 2 * SMALL_FREE_AT, BLOCKS)
            for i in range(QUARTERS):
                k, t = divmod(i, TILES)
                ks = slice(k * HALF, (k + 1) * HALF)
                if t == 0:
                    sp.wait_ge(scaled_act, k + 1)
                else:
                    sp.wait_ge(hn_done, QUARTERS * LAYERS + k + 1)
                sp.dma_start(out_d[:, t, ks], hn[:, t, ks]).then_inc(out_stored, 16)
            sp.wait_ge(out_stored, 16 * QUARTERS)

        @block.gpsimd
        def _(pool):
            for l in range(LAYERS):
                def low_part(b, s, first=False):
                    n = b + l * LAYER
                    pool.wait_ge(whi_done, n + 1)
                    if not first:
                        pool.wait_ge(w_used, n - WLO + 1)
                    nc.gpsimd.tensor_tensor(w_lo[:, s % WLO, :], raw[:, s, :],
                                            whs[:, s].bitcast(F32), ALU.subtract).then_inc(wlo_pool, 1)

                for b in range(RAW):
                    low_part(b, b, first=l == 0 and b < WLO)
                blocks(pool, low_part, RAW, UP_FROM)
            pool.wait_ge(gfin_loaded, 16)
            for k in range(2):
                ks = slice(k * HALF, (k + 1) * HALF)
                pool.wait_ge(x_ready, 8 * LAYERS - 4 + k + 1)
                nc.gpsimd.tensor_tensor(hn[:, 0, ks], xs[:, 0, ks], cnorm[:, ks],
                                        ALU.mult).then_inc(scaled_pool, 1)

        @block.scalar
        def _(act):
            norms, primes = [0], [0]

            def prime(func):
                if primes[0]:
                    act.wait_ge(prime_done, primes[0])
                nc.scalar.activation(primed[:, :], ident[:, 0:1], func).then_inc(prime_done, 1)
                primes[0] += 1

            def norm_stats(src, junk, ready, base):
                norms[0] += 1
                for i in range(QUARTERS):
                    t, k = divmod(i, 2)
                    ks = slice(k * HALF, (k + 1) * HALF)
                    if ready is not None:
                        act.wait_ge(ready, base + i + 1)
                    nc.scalar.activation(junk[:, t, ks], src[:, t, ks], ACT.Square,
                                         accum_out=sumsq[:, k, t:t + 1]).then_inc(sumsq_done, 1)
                act.wait_ge(total_done, norms[0])
                nc.scalar.activation(std[:, :], total[:, :], ACT.Sqrt).then_inc(std_done, 1)

            def high_part(n, s, first=False):
                act.wait_ge(raw_full[s], (n - s) * (16 // RAW) + 16)
                if not first:
                    act.wait_ge(w_used, n - WHI + 1)
                nc.scalar.activation(whs[:, s], raw[:, s, :], ACT.Copy).then_inc(whi_done, 1)

            def high_parts(first, last):
                blocks(act, high_part, first, last)

            def split_chunks(ready, base, bank, scale, chunks=range(DC)):
                for c in chunks:
                    act.wait_ge(ready, base + c // 2 + 1)
                    src = ps[:, bank + c // 2, c % 2 * SEQ:(c % 2 + 1) * SEQ]
                    nc.scalar.activation(hh[:, c, :], src, ACT.Copy, scale=scale(c)).then_inc(hh_done, 1)

            high_part(0, 0, first=True)
            act.wait_ge(consts_loaded, 32)
            for l in range(LAYERS):
                near, far = 4 * l, 4 - 4 * l
                for k in range(2):
                    split_chunks(hT_psum, 8 * l, far, lambda c: gam[:, 2 * l, c:c + 1],
                                 range(k * DC // 2, (k + 1) * DC // 2))
                    if l == 0:
                        for s in range(1 + 2 * k, 3 + k):
                            high_part(s, s, first=True)

                def high(b):
                    high_part(b + l * LAYER, b % RAW)

                high(4)
                high(5)
                prime(ACT.Sqrt)
                norm_stats(xs, hn, None, 0)
                in_norm = norms[0]

                def take_projection(f):
                    act.wait_ge(rinv_done, in_norm)
                    for i in range(QUARTERS):
                        t, k = divmod(i, 2)
                        if i == 0:
                            act.wait_ge(tile_summed, 4 * l + f + 1)
                        elif i == 2:
                            act.wait_ge(w_used, l * LAYER + (f + 1) * DC)
                        src = ps[:, (far if f else near) + 2 * t + k, :]
                        if l == 0:
                            o = f * DM + k * 512
                            nc.scalar.activation(proj[:, t, o:o + 512], src, ACT.Copy,
                                                 scale=rinv[:, 0, t:t + 1]).then_inc(proj_sb, 1)
                        else:
                            dst = (u_sb if f else v_sb)[:, t, k * 512:(k + 1) * 512]
                            nc.scalar.activation(dst, src, ACT.Gelu_apprx_tanh,
                                                 scale=rinv[:, 0, t:t + 1]).then_inc(proj_sb, 1)

                for b in range(6, 12):
                    high(b)
                if l == 0:
                    def exponents(h):
                        act.wait_ge(nmax_done, h + 1)
                        for t in range(TILES):
                            p = probs[:, h, t * SEQ:(t + 1) * SEQ]
                            nc.scalar.activation(p, p, ACT.Exp, bias=rowmax[:, h, t:t + 1],
                                                 accum_out=rowsum[:, h, t:t + 1]).then_inc(exp_done, 1)

                    def take_probsT(h):
                        act.wait_ge(pT_psum, h + 1)
                        nc.scalar.activation(probsT[:, h, :], ps[:, h % 4, :], ACT.Copy).then_inc(pT_sb, 1)

                    take_projection(0)
                    prime(ACT.Exp)
                    for b in (12, 13, 14):
                        high(b)
                    exponents(0)
                    high(15)
                    exponents(1)
                    exponents(2)
                    high(16)
                    exponents(3)
                    high(17)
                    high(18)
                    exponents(4)
                    exponents(5)
                    take_projection(1)
                    exponents(6)
                    high(19)
                    take_probsT(0)
                    take_probsT(1)
                    exponents(7)
                    for g in range(len(WINDOWS)):
                        act.wait_ge(pool_psum, g + 1)
                        nc.scalar.activation(pooledT[:, g, :], ps[:, 4 + g, 0:SEQ],
                                             ACT.Copy).then_inc(pooled_sb, 1)
                    for g in range(len(WINDOWS)):
                        act.wait_ge(poolmix_psum, g + 1)
                        nc.scalar.activation(hh[:, 4 + g, :], ps[:, 4 + g, SEQ:2 * SEQ], ACT.Copy,
                                             scale=pscale[:, g:g + 1]).then_inc(hh_done, 1)
                    take_probsT(2)
                    take_probsT(3)
                    for h in range(4, HEADS):
                        high(16 + h)
                        take_probsT(h)
                    for j in range(HEADS // 2):
                        act.wait_ge(pv_psum, j + 1)
                        nc.scalar.activation(hh[:, j, :], ps[:, j, 0:SEQ], ACT.Copy).then_inc(hh_done, 1)
                else:
                    prime(ACT.Gelu_apprx_tanh)
                    take_projection(0)
                    high(12)
                    prime(ACT.Sqrt)
                    norm_stats(v_sb, vn, proj_sb, 8 * l)
                    for b in range(13, 16):
                        high(b)
                    prime(ACT.Gelu_apprx_tanh)
                    for b in range(16, 19):
                        high(b)
                    take_projection(1)
                    high(19)
                    split_chunks(gT_psum, 0, near, lambda c: 1.0)
                    for b in range(20, Q_FROM):
                        high(b)

                prime(ACT.Sqrt)
                for b in range(Q_FROM, Q_FROM + 3):
                    high(b)
                norm_stats(xs, hn, x_ready, 8 * l)
                high(Q_FROM + 3)
                split_chunks(hT_psum, 8 * l + 4, 4, lambda c: gam[:, 2 * l + 1, c:c + 1])

                def take_queries(f):
                    for i in range(4 * f, 4 * f + 4):
                        if i % 4 < 3:
                            act.wait_ge(q_summed, 6 * l + 3 * f + i % 4 + 1)
                        else:
                            act.wait_ge(w_used, l * LAYER + Q_FROM + (f + 1) * DC)
                        nc.scalar.activation(qT[:, 2 * i:2 * i + 2, :],
                                             ps[:, i, :].rearrange("p (c t) -> p c t", t=SEQ),
                                             ACT.Copy).then_inc(qT_sb, 1)

                high_parts(l * LAYER + Q_FROM + 4, l * LAYER + Q_FROM + 12)
                take_queries(0)
                high_parts(l * LAYER + Q_FROM + 12, l * LAYER + MIX_BLOCKS)
                for b in range(MIX_BLOCKS, MIX_BLOCKS + 3):
                    high(b)
                take_queries(1)
                high(MIX_BLOCKS + 3)
                for i in range(8):
                    act.wait_ge(sc_psum, 8 * l + i + 1)
                    nc.scalar.activation(scores[:, i // 4, i % 4 * 512:(i % 4 + 1) * 512],
                                         ps[:, i, :], ACT.Copy).then_inc(sc_sb, 1)

                def take_hidden(b, s):
                    act.wait_ge(w_used, b + 1 + l * LAYER + MIX_BLOCKS)
                    nc.scalar.activation(arena[:, bass.ds(b * SEQ, SEQ)], ps[:, s, 0:SEQ],
                                         ACT.Gelu_apprx_tanh).then_inc(h_done, 1)

                def activate_hidden(b, s):
                    act.wait_ge(w_used, b + 1 + l * LAYER + MIX_BLOCKS)
                    nc.scalar.activation(ps[:, s, 0:SEQ], ps[:, s, 0:SEQ],
                                         ACT.Gelu_apprx_tanh).then_inc(h_psum, 1)

                def down(b, s):
                    high_part(b + l * LAYER + MIX_BLOCKS, s)
                    take_hidden(b - 2, (s - 2) % RAW)

                def late_down(b, s):
                    high_part(b + l * LAYER + MIX_BLOCKS, s)
                    activate_hidden(b - 2, (s - 2) % RAW)

                prime(ACT.Gelu_apprx_tanh)
                take_hidden(0, 0)
                take_hidden(1, 1)
                blocks(act, down, RAW, EXP_AT)
                act.wait_ge(best_done, l + 1)
                bb = ret[:, BEST_AT:BEST_AT + TILES * P]
                nc.scalar.activation(bb, bb, ACT.Exp).then_inc(gexp_done, 1)
                blocks(act, down, EXP_AT, G_FROM)
                for b in range(G_FROM, G_FROM + RAW):
                    (down if b < G_FROM + 2 else late_down)(b, b % RAW)
                blocks(act, late_down, G_FROM + RAW, BLOCKS)
                def round_hidden(b, s):
                    nc.scalar.activation(hh[:, s, :], arena[:, bass.ds(b * SEQ, SEQ)],
                                         ACT.Copy).then_inc(ghhi_done, 1)

                def up(b, s):
                    high_part(b + l * LAYER + UP_FROM, s)
                    round_hidden(b, s)

                high_part(l * LAYER + UP_FROM, 0)
                activate_hidden(BLOCKS - 2, RAW - 2)
                act.wait_ge(gmul_done, (l + 1) * TGROUPS)
                act.wait_ge(chunks_free, l + 1)
                round_hidden(0, 0)
                high_part(l * LAYER + UP_FROM + 1, 1)
                activate_hidden(BLOCKS - 1, RAW - 1)
                round_hidden(1, 1)
                for b in range(2, RAW):
                    high_part(b + l * LAYER + UP_FROM, b)
                    round_hidden(b, b)
                act.wait_ge(hmul_done, (l + 1) * (BLOCKS - G_FROM))
                blocks(act, up, RAW, BLOCKS)
                if l + 1 < LAYERS:
                    high_parts((l + 1) * LAYER, (l + 1) * LAYER + RAW)
            prime(ACT.Sqrt)
            norm_stats(xs, vn, x_ready, 8 * LAYERS - 4)
            act.wait_ge(rinv_done, norms[0])
            for k in range(2):
                part = hn[:, 0, k * HALF:(k + 1) * HALF]
                act.wait_ge(scaled_pool, k + 1)
                nc.scalar.activation(part, part, ACT.Copy, scale=rinv[:, 0, 0:1]).then_inc(scaled_act, 1)

        @block.tensor
        def _(pe):
            def mm(out, lhsT, rhs, start=True, stop=True, shared=False):
                return nc.tensor.matmul(out, lhsT, rhs, start=start, stop=stop, skip_group_check=shared)

            def transpose_tokens(src, bank, done, pairs=range(DC // 2)):
                for i in pairs:
                    for c in (2 * i, 2 * i + 1):
                        for t in range(TILES):
                            o = (c % 2) * SEQ + t * P
                            last = nc.tensor.transpose(ps[:, bank + i, o:o + P],
                                                       src[:, t, c * P:(c + 1) * P], ident[:, :])
                    last.then_inc(done, 1)


            def high_ready(b, l):
                pe.wait_ge(whi_done, b + 1 + l * LAYER)

            def low_ready(b, l):
                pe.wait_ge(wlo_pool, b + 1 + l * UP_FROM)

            def products(part, c, w, t, banks, start=False, stop=False):
                for k in range(2):
                    last = mm(ps[:, banks + 2 * t + k, :], part[:, c, t * P:(t + 1) * P],
                              w[:, k * HALF:(k + 1) * HALF], start, stop)
                return last

            def tokens_times_block(operand_low, low, c, s, banks, first):
                for t in range(TILES):
                    products(hh, c, whs[:, s], t, banks, start=first)
                pe.wait_ge(*operand_low)
                for t in range(TILES):
                    products(hl, c, whs[:, s], t, banks)
                pe.wait_ge(*low)
                for t in range(TILES):
                    last = products(hh, c, w_lo[:, s % WLO], t, banks)
                last.then_inc(w_used, 1)

            def last_tokens_times_block(operand_low, low, c, s, banks):
                for t in range(TILES):
                    products(hh, c, whs[:, s], t, banks)
                    pe.wait_ge(*operand_low)
                    products(hl, c, whs[:, s], t, banks)
                    pe.wait_ge(*low)
                    products(hh, c, w_lo[:, s % WLO], t, banks, stop=True).then_inc(
                        w_used if t else tile_summed, 1)

            pe.wait_ge(consts_loaded, 32)
            for l in range(LAYERS):
                near, far = 4 * l, 4 - 4 * l

                def transpose_half(src, bank, done, k):
                    transpose_tokens(src, bank, done, range(k * DC // 4, (k + 1) * DC // 4))

                def transpose_halves(src, bank, done, ready, base):
                    for k in range(2):
                        pe.wait_ge(ready, base + TILES * (k + 1))
                        transpose_half(src, bank, done, k)

                def multiply(b, i, c, operand, banks):
                    pe.wait_ge(hh_done, 3 * DC * l + operand)
                    high_ready(b, l)
                    operand_low, low = (hl_done, 3 * DC * l + operand), (wlo_pool, b + 1 + l * UP_FROM)
                    if i < DC - 1:
                        tokens_times_block(operand_low, low, c, b % RAW, banks, i == 0)
                    else:
                        last_tokens_times_block(operand_low, low, c, b % RAW, banks)

                for b in range(IN_BLOCKS):
                    if b == 0 or b == 2:
                        k = b // 2
                        if l == 0:
                            pe.wait_ge(x_loaded[k], 16)
                        else:
                            pe.wait_ge(x_ready, 8 * l - 1 + k)
                        transpose_half(xs, far, hT_psum, k)
                    if b == 0 and l:
                        pe.wait_ge(x_ready, 8 * l)
                    if l == 0:
                        if b == TURN_QK:
                            pe.wait_ge(rot_done, TILES)
                            transpose_tokens(proj, 0, qkT_psum)
                        elif b in SCORE_BEFORE:
                            for h in ((0, 1, 2, 3) if b == SCORE_BEFORE[0] else (4, 5, 6, 7)):
                                if h < 4:
                                    pe.wait_ge(qkT_sb, DC // 2)
                                else:
                                    pe.wait_ge(nmax_done, h - 3)
                                r = slice(h % 2 * HD, (h % 2 + 1) * HD)
                                for t in range(TILES):
                                    last = mm(ps[:, h % 4, t * SEQ:(t + 1) * SEQ],
                                              qkT[r, h // 2, t * P:(t + 1) * P], qkT[r, 4 + h // 2, :])
                                last.then_inc(s_psum, 1)
                    elif b == MIX_BEFORE:
                        pe.wait_ge(sgu_loaded, 48)
                        pe.wait_ge(proj_sb, 12)
                        for t in range(TILES):
                            pe.wait_ge(vn_done, t + 1)
                            for k in range(2):
                                for g in range(4 * k, 4 * k + 4):
                                    o = g % 4 * P
                                    last = mm(ps[:, near + 2 * t + k, o:o + P], ws[:, g, :],
                                              vn[:, t, g * P:(g + 1) * P])
                                last.then_inc(sgu_psum, 1)
                    f, c = divmod(b, DC)
                    if b == DC:
                        pe.wait_ge(hl_done, 3 * DC * l + DC)
                    multiply(b, c, c, DC if f else c + 1, far if f else near)
                if l == 0:
                    def transpose_probs(h):
                        pe.wait_ge(p_done, TILES * (h + 1))
                        if h < 4:
                            pe.wait_ge(nmax_done, h + 5)
                        else:
                            pe.wait_ge(pT_sb, h - 3)
                        for k in range(TILES):
                            for t in range(TILES):
                                o = k * SEQ + t * P
                                last = nc.tensor.transpose(ps[:, h % 4, o:o + P],
                                                           probs[:, h, t * SEQ + k * P:t * SEQ + (k + 1) * P],
                                                           ident[:, :])
                        last.then_inc(pT_psum, 1)

                    transpose_probs(0)
                    transpose_probs(1)
                    pe.wait_ge(proj_sb, 2 * NB)
                    for g in range(len(WINDOWS)):
                        o = 3 * 512 + g * P
                        for t in range(TILES):
                            last = mm(ps[:, 4 + g, 0:SEQ], proj[:, t, o:o + P], poolm[:, t, g, :],
                                      t == 0, t == TILES - 1)
                        last.then_inc(pool_psum, 1)
                    transpose_probs(2)
                    transpose_probs(3)
                    for g in range(len(WINDOWS)):
                        pe.wait_ge(pooled_sb, g + 1)
                        mm(ps[:, 4 + g, SEQ:2 * SEQ], poolw[:, g, :], pooledT[:, g, :]
                           ).then_inc(poolmix_psum, 1)
                    for i in range(len(WINDOWS)):
                        transpose_probs(4 + i)
                        if i == 0:
                            pe.wait_ge(hl_done, DC + len(WINDOWS))
                        multiply(IN_BLOCKS + i, i, 4 + i, DC + len(WINDOWS), far)
                    for j in range(HEADS // 2):
                        pe.wait_ge(pT_sb, j + 5)
                        for h in (2 * j, 2 * j + 1):
                            r = slice(h % 2 * HD, (h % 2 + 1) * HD)
                            for k in range(TILES):
                                v = proj[:, k, 2 * 512 + h * HD:2 * 512 + (h + 1) * HD]
                                last = mm(ps[r, j, 0:SEQ], v, probsT[:, h, k * SEQ:(k + 1) * SEQ],
                                          k == 0, k == TILES - 1)
                        last.then_inc(pv_psum, 1)
                    for j in range(HEADS // 2):
                        multiply(IN_BLOCKS + 4 + j, 4 + j, j, DC + len(WINDOWS) + j + 1, far)
                else:
                    for k in range(2):
                        pe.wait_ge(gated_done, 3 + k)
                        transpose_half(u_sb, near, gT_psum, k)
                    pe.wait_ge(proj_sb, 8 * LAYERS)
                    for c in range(DC):
                        multiply(IN_BLOCKS + c, c, c, DC + c + 1, far)

                transpose_halves(hn, 4, hT_psum, hn_done, QUARTERS * l)
                for b in range(Q_BLOCKS):
                    f, c = divmod(b, DC)
                    operand = DC * (3 * l + 2) + (DC if f else c + 1)
                    pe.wait_ge(hh_done, operand)
                    if b:
                        pe.wait_ge(hl_done, operand)
                    high_ready(Q_FROM + b, l)
                    s = b % RAW

                    def queries(m):
                        return ps[:, 4 * f + m // 2, m % 2 * SEQ:(m % 2 + 1) * SEQ], slice(m * P, (m + 1) * P)

                    def add(m, w, part, start=False, stop=False):
                        out, ms = queries(m)
                        return mm(out, w[:, ms], part[:, c, :], start and m % 2 == 0, stop, shared=True)

                    w = w_lo[:, s % WLO]
                    if c == DC - 1:
                        low_ready(Q_FROM + b, l)
                        for m in range(8):
                            add(m, whs[:, s], hh)
                            add(m, whs[:, s], hl)
                            last = add(m, w, hh, stop=True)
                            if m % 2:
                                last.then_inc(w_used if m == 7 else q_summed, 1)
                        continue
                    if b:
                        for m in range(8):
                            add(m, whs[:, s], hh, start=c == 0)
                            add(m, whs[:, s], hl)
                    else:
                        for m in range(8):
                            add(m, whs[:, s], hh, start=True)
                        pe.wait_ge(hl_done, operand)
                        for m in range(8):
                            add(m, whs[:, s], hl)
                    low_ready(Q_FROM + b, l)
                    for m in range(8):
                        last = add(m, w, hh)
                    last.then_inc(w_used, 1)
                pe.wait_ge(subk_loaded, 16 * (l + 1))
                for t in range(TILES):
                    for n in range(HALVES):
                        if n % 4 == 0:
                            pe.wait_ge(qT_sb, 8 * l + (8 if t else max(4, n // 2 + 2)))
                        o = n % 4 * P
                        last = mm(ps[:, 4 * t + n // 4, o:o + P], qT[:, n, t * P:(t + 1) * P], subk[:, n, :])
                        if n % 4 == 3:
                            last.then_inc(sc_psum, 1)

                def down(b, s, when="early", final=False):
                    high_ready(b + MIX_BLOCKS, l)
                    if when == "first":
                        pe.wait_ge(sc_sb, 8 * l + s + 1)
                    elif when == "early":
                        pe.wait_ge(h_done, b - RAW + 1 + l * G_FROM)
                    else:
                        pe.wait_ge(hmul_done, b - RAW + 1 - G_FROM + l * (BLOCKS - G_FROM))
                    out = ps[:, s, 0:SEQ]
                    for c in range(DC):
                        cs = slice(c * P, (c + 1) * P)
                        mm(out, whs[:, s, cs], hh[:, c, :], c == 0, False)
                        mm(out, whs[:, s, cs], hl[:, c, :], False, False)
                    low_ready(b + MIX_BLOCKS, l)
                    for c in range(DC):
                        last = mm(out, w_lo[:, s % WLO, c * P:(c + 1) * P], hh[:, c, :], False, c == DC - 1)
                        if final and c == RAW - 1:
                            last.then_inc(chunks_free, 1)
                    last.then_inc(w_used, 1)

                for b in range(RAW):
                    down(b, b, "first")
                blocks(pe, down, RAW, IDS_AT)
                pe.wait_ge(sc_sb, 8 * (l + 1))
                pe.wait_ge(idg_done, l + 1)
                for t in range(TILES):
                    nc.tensor.transpose(ps[:, 4, t * P:(t + 1) * P],
                                        ret[:, BEST_AT + t * P:BEST_AT + (t + 1) * P], ident[:, :])
                for t in range(TILES):
                    last = nc.tensor.transpose(ps[:, 4, SEQ + t * P:SEQ + (t + 1) * P], idf[:, t, :],
                                               ident[:, :])
                last.then_inc(idg_psum, 1)
                blocks(pe, down, IDS_AT, G_FROM)

                def token_gates(g, s, first=False):
                    pe.wait_ge(oh_built, (g + 1 + l * TGROUPS) * (TOK + 1))
                    if not first:
                        pe.wait_ge(gmul_done, g - 3 + l * TGROUPS)
                    for k in range(TOK):
                        last = mm(ps[:, 4 + s, k * P:(k + 1) * P], oh2[:, s % 2, k, :], oh1g[:, s % 2, k, :])
                    last.then_inc(g_mm, 1)

                for j in range(RAW):
                    down(G_FROM + j, j)
                    token_gates(j, j, first=True)
                with pe.Fori(1, TGROUPS // RAW) as i:
                    for j in range(RAW):
                        down(G_FROM + i * RAW + j, j, "late")
                        token_gates(i * RAW + j, j)
                blocks(pe, lambda b, s: down(b, s, "late"), G_TO, BLOCKS - RAW)
                for b in range(BLOCKS - RAW, BLOCKS):
                    down(b, b % RAW, "late", final=b == BLOCKS - 1)

                def up(b, s, first=False, final=False):
                    high_ready(b + UP_FROM, l)
                    pe.wait_ge(ghhi_done, b + l * BLOCKS + 1)
                    operand_low, low = (ghlo_done, b + l * BLOCKS + 1), (wlo_dve, b + l * BLOCKS + 1)
                    if final:
                        last_tokens_times_block(operand_low, low, s, s, 4)
                    else:
                        tokens_times_block(operand_low, low, s, s, 4, first)

                for b in range(RAW):
                    up(b, b, first=b == 0)
                blocks(pe, up, RAW, BLOCKS - RAW)
                for b in range(BLOCKS - RAW, BLOCKS):
                    up(b, b % RAW, final=b == BLOCKS - 1)

        @block.vector
        def _(dve):
            steps = [0]
            norms, sums = [0], [0]

            def step(ins):
                steps[0] += 1
                return ins.then_inc(dve_step, 1)

            def settle():
                dve.wait_ge(dve_step, steps[0])

            def norm_scale(kind):
                norms[0] += 1
                r = rinv[:, kind, :]
                dve.wait_ge(sumsq_done, QUARTERS * norms[0])
                nc.vector.scalar_tensor_tensor(total[:, :], sumsq[:, 0, :], DM * EPS, sumsq[:, 1, :],
                                               ALU.add, ALU.add).then_inc(total_done, 1)
                dve.wait_ge(std_done, norms[0])
                step(nc.vector.reciprocal(r, std[:, :]))
                settle()
                step(nc.vector.scalar_tensor_tensor(rtmp[:, :], r, -0.5 * DM ** 0.5, r, ALU.mult, ALU.mult))
                settle()
                step(nc.vector.tensor_tensor(rtmp[:, :], rtmp[:, :], total[:, :], ALU.mult))
                settle()
                nc.vector.scalar_tensor_tensor(r, rtmp[:, :], 1.5 * DM ** 0.5, r, ALU.add,
                                               ALU.mult).then_inc(rinv_done, 1)
                dve.wait_ge(rinv_done, norms[0])

            def norm_tokens():
                norm_scale(2)
                for i in range(QUARTERS):
                    k, t = divmod(i, TILES)
                    ks = slice(k * HALF, (k + 1) * HALF)
                    nc.vector.tensor_scalar(hn[:, t, ks], xs[:, t, ks], rinv[:, 2, t:t + 1], None,
                                            ALU.mult).then_inc(hn_done, 1)

            hh_seen = [0]

            def split_chunks(chunks, bank_of, scale):
                for i, c in enumerate(chunks):
                    hh_need = hh_seen[0] + (i // 2 * 2 + 2)
                    dve.wait_ge(hh_done, hh_need)
                    bank, o = bank_of(c)
                    src = ps[:, bank, o:o + SEQ]
                    if scale is None:
                        ins = nc.vector.tensor_tensor(hl[:, c, :], src, hh[:, c, :].bitcast(F32), ALU.subtract)
                    else:
                        ins = nc.vector.scalar_tensor_tensor(hl[:, c, :], src, scale(c),
                                                             hh[:, c, :].bitcast(F32), ALU.mult, ALU.subtract)
                    ins.then_inc(hl_done, 1)
                hh_seen[0] += len(chunks)

            def paired(bank):
                return lambda c: (bank + c // 2, c % 2 * SEQ)

            def add_residual(done, count, bank):
                sums[0] += 1
                tiles = 4 * ((sums[0] - 1) // 2) + 3 + (sums[0] - 1) % 2
                for i in range(QUARTERS):
                    t, k = divmod(i, 2)
                    if i == 0:
                        dve.wait_ge(tile_summed, tiles)
                    elif i == 2:
                        dve.wait_ge(done, count)
                    part = xs[:, t, k * HALF:(k + 1) * HALF]
                    nc.vector.tensor_tensor(part, part, ps[:, bank + 2 * t + k, :],
                                            ALU.add).then_inc(x_ready, 1)

            dve.wait_ge(consts_loaded, 32)
            for l in range(LAYERS):
                near, far = 4 * l, 4 - 4 * l
                split_chunks(range(DC), paired(far), lambda c: gam[:, 2 * l, c:c + 1])
                norm_scale(0)
                if l == 0:
                    dve.wait_ge(tabs_loaded, 112)
                    for t in range(TILES):
                        dve.wait_ge(proj_sb, 2 * (t + 1))
                        qk = proj[:, t, 0:2 * 512].rearrange("p (h d) -> p h d", d=HD)
                        t1, t2 = qk[:, :, 0:ROT], qk[:, :, ROT:2 * ROT]
                        cos = tab[:, 0, t, :].unsqueeze(1).to_broadcast([P, 2 * HEADS, ROT])
                        sin = tab[:, 1, t, :].unsqueeze(1).to_broadcast([P, 2 * HEADS, ROT])
                        if t:
                            dve.wait_ge(rot_done, t)
                        step(nc.vector.tensor_tensor(rot[:, 0], t1, cos, ALU.mult))
                        step(nc.vector.tensor_tensor(rot[:, 1], t2, sin, ALU.mult))
                        step(nc.vector.tensor_tensor(rot[:, 2], t2, cos, ALU.mult))
                        step(nc.vector.tensor_tensor(rot[:, 3], t1, sin, ALU.mult))
                        settle()
                        step(nc.vector.tensor_tensor(t1, rot[:, 0], rot[:, 1], ALU.subtract))
                        settle()
                        nc.vector.tensor_tensor(t2, rot[:, 2], rot[:, 3], ALU.add).then_inc(rot_done, 1)
                    for i in range(DC // 2):
                        dve.wait_ge(qkT_psum, i + 1)
                        nc.vector.tensor_copy(qkT[:, 2 * i:2 * i + 2, :],
                                              ps[:, i, :].rearrange("p (c t) -> p c t", t=SEQ)
                                              ).then_inc(qkT_sb, 1)
                    def weigh(h):
                        dve.wait_ge(s_psum, h + 1)
                        step(nc.vector.scalar_tensor_tensor(probs[:, h, :], ps[:, h % 4, :], HD ** -0.5,
                                                            lncount, ALU.mult, ALU.add))
                        settle()
                        step(nc.vector.reduce_max(rowmax[:, h, :], probs[:, h, :].rearrange(
                            "p (t k) -> p t k", k=SEQ), AX.X))
                        settle()
                        nc.vector.tensor_scalar(rowmax[:, h, :], rowmax[:, h, :], -1.0, None,
                                                ALU.mult).then_inc(nmax_done, 1)

                    def normalise(h):
                        dve.wait_ge(exp_done, TILES * (h + 1))
                        step(nc.vector.reciprocal(rowinv[:, h, :], rowsum[:, h, :]))
                        settle()
                        for t in range(TILES):
                            p = probs[:, h, t * SEQ:(t + 1) * SEQ]
                            nc.vector.tensor_scalar(p, p, rowinv[:, h, t:t + 1], None,
                                                    ALU.mult).then_inc(p_done, 1)

                    for h in range(4):
                        weigh(h)
                    for h in range(4):
                        normalise(h)
                    for h in range(4, HEADS):
                        weigh(h)
                        if h > 4:
                            normalise(h - 1)
                    normalise(HEADS - 1)
                    for g in range(len(WINDOWS)):
                        dve.wait_ge(hh_done, hh_seen[0] + g + 1)
                        nc.vector.scalar_tensor_tensor(
                            hl[:, 4 + g, :], ps[:, 4 + g, SEQ:2 * SEQ], pscale[:, g:g + 1],
                            hh[:, 4 + g, :].bitcast(F32), ALU.mult, ALU.subtract).then_inc(hl_done, 1)
                    hh_seen[0] += len(WINDOWS)

                    for j in range(HEADS // 2):
                        dve.wait_ge(hh_done, hh_seen[0] + j + 1)
                        nc.vector.tensor_tensor(hl[:, j, :], ps[:, j, 0:SEQ], hh[:, j, :].bitcast(F32),
                                                ALU.subtract).then_inc(hl_done, 1)
                    hh_seen[0] += HEADS // 2
                else:
                    norm_scale(1)
                    dve.wait_ge(sgu_loaded, 48)
                    for t in range(TILES):
                        nc.vector.scalar_tensor_tensor(vn[:, t, :], v_sb[:, t, :], rinv[:, 1, t:t + 1], cnorm,
                                                       ALU.mult, ALU.mult).then_inc(vn_done, 1)
                    for i in range(QUARTERS):
                        t, k = divmod(i, 2)
                        dve.wait_ge(sgu_psum, i + 1)
                        bias = bs[:, 4 * k:4 * k + 4].unsqueeze(2).to_broadcast([P, 4, P])
                        step(nc.vector.tensor_tensor(
                            vn[:, t, k * HALF:(k + 1) * HALF].rearrange("p (g c) -> p g c", c=P),
                            ps[:, near + i, :].rearrange("p (g c) -> p g c", c=P), bias, ALU.add))
                    settle()
                    for i in range(QUARTERS):
                        t, k = divmod(i, 2)
                        ks = slice(k * HALF, (k + 1) * HALF)
                        dve.wait_ge(proj_sb, 12 + i + 1)
                        nc.vector.tensor_tensor(u_sb[:, t, ks], u_sb[:, t, ks], vn[:, t, ks],
                                                ALU.mult).then_inc(gated_done, 1)
                    split_chunks(range(DC), paired(near), None)
                add_residual(w_used, l * LAYER + Q_FROM, far)

                dve.wait_ge(x_ready, 8 * l + 4)
                norm_tokens()
                split_chunks(range(DC), paired(4), lambda c: gam[:, 2 * l + 1, c:c + 1])

                def top16(rows):
                    for r in range(0, len(rows), 4):
                        some = rows[r:r + 4]
                        for half in (slice(0, 8), slice(8, 16)):
                            settle()
                            for vals, top, pos in some:
                                step(nc.vector.max(top[:, half], vals))
                            settle()
                            for vals, top, pos in some:
                                step(nc.vector.max_index(pos[:, half], top[:, half], vals))
                            if half.start == 0:
                                settle()
                                for vals, top, pos in some:
                                    step(nc.vector.match_replace(vals, top[:, half], vals, LOWEST))

                for t in range(TILES):
                    dve.wait_ge(sc_sb, 8 * l + 4 * (t + 1))
                    top16([(scores[:, t, n * KEYS:(n + 1) * KEYS], sv[:, t, n, :], si[:, t, n, :])
                           for n in range(HALVES)])
                    settle()
                    step(nc.vector.tensor_copy(sif[:, t].rearrange("p h i k -> p (h i) k"), si[:, t]))
                    settle()
                    step(nc.vector.tensor_scalar(sif[:, t, :, 0, :], sif[:, t, :, 0, :], float(KEYS), None,
                                                 ALU.mult))
                    settle()
                    svt = sv[:, t].rearrange("p (h i) k -> p h i k", i=2)
                    o = 0
                    for a0, a1, nb in SEGS:
                        na = a1 - a0
                        for dst, src in ((cand, svt), (pay, sif[:, t])):
                            d = dst[:, :, o:o + na * nb].rearrange("p h (a b) -> p h a b", b=nb)
                            f = src[:, :, 0, a0:a1].unsqueeze(3).to_broadcast([P, RH, na, nb])
                            s = src[:, :, 1, 0:nb].unsqueeze(2).to_broadcast([P, RH, na, nb])
                            step(nc.vector.tensor_tensor(d, f, s, ALU.add))
                        o += na * nb
                    top16([(cand[:, h, :], best[:, t, h, :], ci[:, t, h, :]) for h in range(RH)])
                    settle()
                    step(nc.vector.tensor_copy(cif[:, t], ci[:, t].rearrange("p h k -> p (h k)")))
                    settle()
                    for h in range(0, RH, 2):
                        n = 2 * TOPK
                        step(nc.vector.tensor_tensor(
                            eq, iotac[:, :].unsqueeze(1).to_broadcast([P, n, CAND]),
                            cif[:, t, h * TOPK:h * TOPK + n].unsqueeze(2).to_broadcast([P, n, CAND]),
                            ALU.is_equal))
                        settle()
                        e4 = eq.rearrange("p (h k) c -> p h k c", k=TOPK)
                        step(nc.vector.tensor_tensor(
                            e4, e4, pay[:, h:h + 2, :].unsqueeze(2).to_broadcast([P, 2, TOPK, CAND]),
                            ALU.mult))
                        settle()
                        step(nc.vector.reduce_sum(idf[:, t, h * TOPK:h * TOPK + n], eq, AX.X))
                        settle()
                b3 = best.rearrange("p t h k -> p (t h) k")
                gs = gsum[:, :, :].rearrange("p a h -> p (a h)")
                top, tot = gs[:, 0:TILES * RH], gs[:, TILES * RH:2 * TILES * RH]
                wide = [P, TILES * RH, TOPK]
                step(nc.vector.tensor_copy(top, b3[:, :, 0]))
                settle()
                nc.vector.tensor_tensor(b3, b3, top.unsqueeze(2).to_broadcast(wide),
                                        ALU.subtract).then_inc(best_done, 1)
                dve.wait_ge(gexp_done, l + 1)
                step(nc.vector.reduce_sum(tot, b3, AX.X))
                settle()
                step(nc.vector.reciprocal(tot, tot))
                settle()
                nc.vector.tensor_tensor(b3, b3, tot.unsqueeze(2).to_broadcast(wide),
                                        ALU.mult).then_inc(idg_done, 1)
                settle()
                step(nc.vector.memset(arena[:, G_FROM * SEQ:BLOCKS * SEQ], 1.0))
                dve.wait_ge(idg_psum, l + 1)
                step(nc.vector.tensor_copy(gT, ps[:, 4, 0:SEQ]))
                step(nc.vector.tensor_copy(idi, ps[:, 4, SEQ:2 * SEQ]))
                settle()
                step(nc.vector.tensor_scalar(idk, idi, 7, None, ALU.arith_shift_right))
                settle()
                step(nc.vector.tensor_copy(i1T, idk))
                step(nc.vector.tensor_scalar(idi, idi, KEYS - 1, None, ALU.bitwise_and))
                settle()
                step(nc.vector.tensor_copy(i2T, idi))
                settle()

                def low_part(b, s):
                    n = b + l * LAYER + UP_FROM
                    dve.wait_ge(whi_done, n + 1)
                    dve.wait_ge(w_used, n - WLO + 1)
                    nc.vector.tensor_tensor(w_lo[:, s % WLO, :], raw[:, s, :], whs[:, s].bitcast(F32),
                                            ALU.subtract).then_inc(wlo_dve, 1)

                gates_before, hiddens_before = l * TGROUPS, l * (BLOCKS - G_FROM)

                def build_first(g, s, first=False):
                    if not first:
                        dve.wait_ge(g_mm, g - 1 + gates_before)
                    for k in range(TOK):
                        t = bass.ds(g * TOK + k, 1)
                        nc.vector.tensor_scalar(oh1g[:, s, k, :], iota[:, :], i1T[:, t], gT[:, t],
                                                ALU.is_equal, ALU.mult).then_inc(oh_built, 1)

                def build_second(g, s):
                    keys = i2T[:, bass.ds(g * TOK, TOK)].unsqueeze(2).to_broadcast([P, TOK, P])
                    nc.vector.tensor_tensor(oh2[:, s], iota3, keys, ALU.is_equal).then_inc(oh_built, 1)

                def gate(g, s, hiddens):
                    dve.wait_ge(g_mm, g + 1 + gates_before)
                    if hiddens is not None:
                        dve.wait_ge(hmul_done, hiddens + hiddens_before)
                    part = H[:, :, bass.ds(g * TOK, TOK)]
                    nc.vector.tensor_tensor(part, part, ps[:, 4 + s, :].rearrange("p (t i) -> p i t", t=TOK),
                                            ALU.mult).then_inc(gmul_done, 1)

                def hidden(b, s, gates=TGROUPS):
                    dve.wait_ge(h_psum, b - G_FROM + 1 + hiddens_before)
                    dve.wait_ge(gmul_done, gates + gates_before)
                    part = arena[:, bass.ds(b * SEQ, SEQ)]
                    nc.vector.tensor_tensor(part, part, ps[:, s, 0:SEQ], ALU.mult).then_inc(hmul_done, 1)

                def turn(g, j):
                    build_first(g + 1, (j + 1) % 2)
                    hidden(g + (G_FROM - 2), (j - 2) % RAW, gates=g)
                    build_second(g + 1, (j + 1) % 2)
                    gate(g, j, hiddens=g - 1)

                build_first(0, 0, first=True)
                build_second(0, 0)
                build_first(1, 1, first=True)
                build_second(1, 1)
                dve.wait_ge(h_done, (l + 1) * G_FROM)
                gate(0, 0, None)
                build_first(2, 0)
                build_second(2, 0)
                gate(1, 1, None)
                turn(2, 2)
                turn(3, 3)
                with dve.Fori(1, TGROUPS // RAW - 1) as i:
                    for j in range(RAW):
                        turn(i * RAW + j, j)
                for g in range(TGROUPS - RAW, TGROUPS - 1):
                    turn(g, g % RAW)
                hidden(G_TO - 3, (G_TO - 3) % RAW, gates=TGROUPS - 1)
                gate(TGROUPS - 1, (TGROUPS - 1) % RAW, hiddens=TGROUPS - 2)
                blocks(dve, lambda b, s: hidden(b - 2, (s - 2) % RAW), G_TO, BLOCKS)
                low_part(0, 0)
                hidden(BLOCKS - 2, RAW - 2)

                def low_hidden(b, s):
                    dve.wait_ge(ghhi_done, b + l * BLOCKS + 1)
                    nc.vector.tensor_tensor(hl[:, s, :], arena[:, bass.ds(b * SEQ, SEQ)],
                                            hh[:, s, :].bitcast(F32), ALU.subtract).then_inc(ghlo_done, 1)

                def up(b, s):
                    low_part(b, s)
                    low_hidden(b, s)

                low_hidden(0, 0)
                low_part(1, 1)
                hidden(BLOCKS - 1, RAW - 1)
                low_hidden(1, 1)
                for b in range(2, RAW):
                    up(b, b)
                blocks(dve, up, RAW, BLOCKS)
                add_residual(w_used, (l + 1) * LAYER, 4)
            dve.wait_ge(x_ready, 8 * LAYERS)
            norm_scale(0)
            dve.wait_ge(gfin_loaded, 16)
            for k in range(2):
                ks = slice(k * HALF, (k + 1) * HALF)
                nc.vector.scalar_tensor_tensor(hn[:, 1, ks], xs[:, 1, ks], rinv[:, 0, 1:2], cnorm[:, ks],
                                               ALU.mult, ALU.mult).then_inc(hn_done, 1)


def shape_tables():
    f = np.float32
    pos = np.arange(SEQ, dtype=f)
    inv = (f(500000.0) ** (-np.arange(0, 2 * ROT, 2, dtype=f) / f(2 * ROT))).astype(f)
    ang = (pos[:, None] * inv[None, :]).astype(f)
    tab = np.stack([np.cos(ang), np.sin(ang)]).astype(f).reshape(2, TILES, P, ROT).transpose(2, 0, 1, 3)
    rel = np.abs(np.arange(SEQ)[:, None] - np.arange(SEQ)[None, :])
    count = sum(((rel % dil == 0) & (rel <= window // 2)).astype(np.float64) for window, dil in PATTERNS)
    lncount = np.where(count > 0, np.log(np.maximum(count, 1)), -1e30).astype(f)
    lncount = lncount.reshape(TILES, P, SEQ).transpose(1, 0, 2).reshape(P, TILES * SEQ)
    poolm = np.zeros((SEQ, len(WINDOWS), SEQ), f)
    for g, win in enumerate(WINDOWS):
        for t in range(SEQ):
            lo, hi = max(t - win // 2, 0), min(t + win - win // 2, SEQ)
            poolm[lo:hi, g, t] = 1.0 / (hi - lo)
            poolm[t, g, t] -= 1.0
    poolm = poolm.reshape(TILES, P, len(WINDOWS), SEQ).transpose(1, 0, 2, 3)
    ones = np.ones((P, 1), f)
    return {"tab": tab, "lncount": lncount, "poolm": poolm, "ident": np.eye(P, dtype=f),
            "iota": ones * np.arange(P, dtype=f), "iotac": ones * np.arange(CAND, dtype=f)}


def kernel(**inputs):
    import numpy as _np
    import concourse.bacc as _bacc
    from concourse import mybir as _mybir
    from concourse.bass_utils import run_bass_kernel_spmd as _run

    a = {k: _np.asarray(v) for k, v in inputs.items()}

    def column_blocks(w):
        w = w.reshape(LAYERS, DC, P, -1, DM).transpose(0, 3, 1, 2, 4)
        return w.reshape(LAYERS, -1, P, DM)

    v_first = _np.concatenate([a["c_w_in"][:, :, DM:], a["c_w_in"][:, :, :DM]], axis=2)
    half = DM // 2
    pooled_first = _np.concatenate([a["ab_w_out"][:, half:], a["ab_w_out"][:, :half]], axis=1)
    gammas = _np.stack([a["norm_mix"], a["norm_ffn"]], axis=1).reshape(2 * LAYERS, DC, P)
    arrays = {
        "x": a["x"].reshape(TILES, P, DM).transpose(1, 0, 2),
        "gam": gammas.transpose(2, 0, 1),
        "gfin": _np.broadcast_to(a["norm_final"], (P, DM)),
        **shape_tables(),
        "poolw": a["pool_w"][0].transpose(1, 0, 2),
        "pscale": a["pool_scale"].reshape(len(WINDOWS), P).transpose(1, 0),
        "wm": _np.concatenate([column_blocks(_np.concatenate([a["ab_w_in"], v_first])),
                               column_blocks(_np.concatenate([pooled_first, a["c_w_out"]])),
                               column_blocks(a["peer_w_q"])], axis=1),
        "ws": a["c_w_s"][0].transpose(2, 0, 1),
        "bs": a["c_b_s"][0].transpose(1, 0),
        "cnorm": _np.broadcast_to(a["c_norm"].reshape(DM), (P, DM)),
        "subk": a["peer_sub_keys"].reshape(LAYERS, HALVES, KEYS, P).transpose(0, 3, 1, 2),
        "wd": a["peer_w_down"].reshape(LAYERS, BLOCKS, KEYS, DC, P).transpose(0, 1, 4, 3, 2).reshape(
            LAYERS, BLOCKS, P, DM),
        "wu": a["peer_w_up"].reshape(LAYERS, BLOCKS, KEYS, DM),
    }
    order = ["x", "gam", "gfin", "tab", "ident", "iota", "iotac", "lncount", "poolm", "poolw", "pscale",
             "wm", "ws", "bs", "cnorm", "subk", "wd", "wu"]
    nc = _bacc.Bacc("TRN2", target_bir_lowering=False, num_devices=1)
    feeds, args = {}, []
    for name in order:
        arr = _np.ascontiguousarray(arrays[name])
        feeds[f"in_{name}"] = arr
        args.append(nc.dram_tensor(f"in_{name}", arr.shape, _mybir.dt.from_np(arr.dtype),
                                   kind="ExternalInput").ap())
    out = nc.dram_tensor("out", (P, TILES, DM), _mybir.dt.float32, kind="ExternalOutput").ap()
    build_trunk(nc, *args, out)
    r = _run(nc, [feeds], core_ids=[0])
    return r.results[0]["out"].transpose(1, 0, 2).reshape(1, SEQ, DM)
```
